# Optimizing a Trainium2 kernel written in Bass

```python
import math
import jax, jax.numpy as jnp
from jax import lax
import numpy as np

D_MODEL = 2048
BATCH = 1
SEQ = 256
DEPTH = 1
DEC_BATCH = 8
DEC_SEQ = 4
PAST_LEN = 2048
PAGE_SIZE = 128

A_HEADS = 8
A_DK = 128
A_DV = 128
A_KEY_WIDTH = A_HEADS * A_DK
A_WIDTH = A_HEADS * A_DV
HGRN_CHUNK = 64
B_HEADS = 16
B_KV_HEADS = 4
B_GROUP = B_HEADS // B_KV_HEADS
B_HD = 64
B_WIDTH = B_HEADS * B_HD
B_KV_WIDTH = B_KV_HEADS * B_HD
WINDOW = 128
ATTN_SCALE = 1.0 / math.sqrt(B_HD)
NEG_LOGIT = -1e30
LB_FLOOR = 1e-20
N_BUCKETS = 32
MAX_DISTANCE = 128
MIX_WIDTH = A_WIDTH + B_WIDTH
SPLIT_POINTS = (A_KEY_WIDTH,
                2 * A_KEY_WIDTH,
                2 * A_KEY_WIDTH + A_WIDTH,
                2 * A_KEY_WIDTH + 2 * A_WIDTH,
                2 * A_KEY_WIDTH + 2 * A_WIDTH + B_WIDTH,
                2 * A_KEY_WIDTH + 2 * A_WIDTH + B_WIDTH + B_KV_WIDTH)
IN_WIDTH = 2 * A_KEY_WIDTH + 2 * A_WIDTH + B_WIDTH + 2 * B_KV_WIDTH
D_FF = ((8 * D_MODEL // 3 + 255) // 256) * 256
RMS_EPS = 1e-6

kernel_name = 'hymba_hgrn2_swa_sink_decoder_step'

def rms_norm(x, g):
    xf = x.astype(jnp.float32)
    y = xf * lax.rsqrt(jnp.mean(xf * xf, axis=-1, keepdims=True) + RMS_EPS)
    return (y * g.astype(jnp.float32)).astype(x.dtype)

def t5_bucket(dist):
    n = np.maximum(dist, 0)
    max_exact = N_BUCKETS // 2
    nf = np.maximum(n, 1).astype(np.float32)
    large = max_exact + (np.log(nf / max_exact) / math.log(MAX_DISTANCE / max_exact)
                         * (N_BUCKETS - max_exact)).astype(np.int32)
    large = np.minimum(large, N_BUCKETS - 1)
    return np.where(n < max_exact, n, large).astype(np.int32)

def relative_bias(table, dist):
    b = table.astype(jnp.float32)[t5_bucket(dist)]
    return jnp.transpose(b, (2, 0, 1)).reshape(B_KV_HEADS, B_GROUP, dist.shape[0], dist.shape[1])

def sink_softmax(s, sink):
    sk = sink.astype(jnp.float32).reshape(B_KV_HEADS, B_GROUP, 1, 1)
    m = jnp.maximum(jnp.max(s, axis=-1, keepdims=True), sk)
    e = jnp.exp(s - m)
    return e / (jnp.sum(e, axis=-1, keepdims=True) + jnp.exp(sk - m))

def hgrn2_scan(q, log_f, k, v, s0):
    bsz, length = q.shape[0], q.shape[1]
    c = min(HGRN_CHUNK, length)
    n = -(-length // c)
    pad = n * c - length

    def blocks(t):
        t = jnp.pad(t, ((0, 0), (0, pad), (0, 0), (0, 0)))
        return t.reshape(bsz, n, c, t.shape[2], t.shape[3]).transpose(1, 0, 3, 2, 4)

    causal = jnp.asarray(np.tril(np.ones((c, c), dtype=bool)))[:, :, None]

    def step(state, inp):
        qc, lfc, kc, vc = inp
        b = jnp.cumsum(lfc, axis=2)
        o_inter = jnp.einsum('bhtk,bhkv->bhtv', qc * jnp.exp(b), state)
        diff = b[:, :, :, None, :] - b[:, :, None, :, :]
        decay = jnp.where(causal, jnp.exp(jnp.where(causal, diff, 0.0)), 0.0)
        a = jnp.einsum('bhtk,bhtsk,bhsk->bhts', qc, decay, kc)
        o_intra = jnp.einsum('bhts,bhsv->bhtv', a, vc)
        b_last = b[:, :, -1:, :]
        new_state = (jnp.exp(b_last[:, :, 0, :])[..., None] * state
                     + jnp.einsum('bhsk,bhsv->bhkv', kc * jnp.exp(b_last - b), vc))
        return new_state, o_inter + o_intra

    s_final, o = lax.scan(step, s0, (blocks(q), blocks(log_f), blocks(k), blocks(v)))
    o = o.transpose(1, 0, 3, 2, 4).reshape(bsz, n * c, q.shape[2], v.shape[3])[:, :length]
    return o, s_final

def mixer_inputs(x, norm_g, w_in, lb, qn_g, kn_g):
    bsz, length, _ = x.shape
    u = rms_norm(x, norm_g) @ w_in
    qa, fa, ia, ga, qb, kb, vb = jnp.split(u, SPLIT_POINTS, axis=-1)
    z = fa.astype(jnp.float32)
    log_lb = jnp.log(jnp.maximum(lb, LB_FLOOR))
    log_f = jnp.logaddexp(log_lb, jnp.log1p(-lb) + jax.nn.log_sigmoid(z))
    ka = (1.0 - lb) * jax.nn.sigmoid(-z)
    qa = jax.nn.silu(qa.astype(jnp.float32))
    a_shape = (bsz, length, A_HEADS, A_DK)
    hgrn = (qa.reshape(a_shape), log_f.reshape(a_shape), ka.reshape(a_shape),
            ia.astype(jnp.float32).reshape(bsz, length, A_HEADS, A_DV), ga)
    qb = rms_norm(qb.reshape(bsz, length, B_HEADS, B_HD), qn_g)
    kb = rms_norm(kb.reshape(bsz, length, B_KV_HEADS, B_HD), kn_g)
    vb = vb.reshape(bsz, length, B_KV_HEADS, B_HD)
    return hgrn, (qb, kb, vb)

def hgrn2_output(o, gn, ga, dtype):
    bsz, length = o.shape[0], o.shape[1]
    gate = jax.nn.silu(ga.astype(jnp.float32)).reshape(bsz, length, A_HEADS, A_DV)
    return (rms_norm(o, gn) * gate).reshape(bsz, length, A_WIDTH).astype(dtype)

def swa_prompt(q, k, v, sink, bias, mask):
    bsz, length = q.shape[0], q.shape[1]
    nb = length // WINDOW
    qb = q.reshape(bsz, nb, WINDOW, B_KV_HEADS, B_GROUP, B_HD)

    def band(t):
        t = t.reshape(bsz, nb, WINDOW, B_KV_HEADS, B_HD)
        prev = jnp.concatenate([jnp.zeros_like(t[:, :1]), t[:, :-1]], axis=1)
        return jnp.concatenate([prev, t], axis=2)

    kb, vb = band(k), band(v)
    s = jnp.einsum('bnqhgd,bnshd->bnhgqs', qb, kb, preferred_element_type=jnp.float32) * ATTN_SCALE + bias
    s = jnp.where(mask[None, :, None, None], s, NEG_LOGIT)
    p = sink_softmax(s, sink)
    o = jnp.einsum('bnhgqs,bnshd->bnqhgd', p.astype(v.dtype), vb)
    return o.reshape(bsz, length, B_WIDTH)

def swa_sample(q, k, v, ck, cv, sink, bias, mask):
    bsz, length = q.shape[0], q.shape[1]
    w = ck.shape[1]
    kall = jnp.concatenate([ck.astype(k.dtype), k], axis=1)
    vall = jnp.concatenate([cv.astype(v.dtype), v], axis=1)
    q5 = q.reshape(bsz, length, B_KV_HEADS, B_GROUP, B_HD)
    s = jnp.einsum('blhgd,bshd->bhgls', q5, kall, preferred_element_type=jnp.float32) * ATTN_SCALE + bias
    s = jnp.where(mask, s, NEG_LOGIT)
    p = sink_softmax(s, sink)
    o = jnp.einsum('bhgls,bshd->blhgd', p.astype(vall.dtype), vall).reshape(bsz, length, B_WIDTH)
    return o, kall[:, -w:], vall[:, -w:]

def swiglu(x, g, wg, wu, wd):
    h = rms_norm(x, g)
    return x + (jax.nn.silu(h @ wg) * (h @ wu)) @ wd

def setup_inputs(seed: int = 0) -> dict:
    key = jax.random.key(seed)
    ks = jax.random.split(key, 20)
    w = min(WINDOW, PAST_LEN)

    def nrm(k, shape, scale):
        return scale * jax.random.normal(k, shape, jnp.float32)

    return {
        'x_prompt': nrm(ks[0], (BATCH, SEQ, D_MODEL), 1.0),
        'x_sample': nrm(ks[1], (DEC_BATCH, DEC_SEQ, D_MODEL), 1.0),
        'cache_k': nrm(ks[2], (DEPTH, DEC_BATCH, w, B_KV_HEADS, B_HD), 1.0),
        'cache_v': nrm(ks[3], (DEPTH, DEC_BATCH, w, B_KV_HEADS, B_HD), 1.0),
        'state_hgrn': nrm(ks[4], (DEPTH, DEC_BATCH, A_HEADS, A_DK, A_DV), 0.5),
        'norm_mix': 1.0 + nrm(ks[5], (DEPTH, D_MODEL), 0.02),
        'w_in': nrm(ks[6], (DEPTH, D_MODEL, IN_WIDTH), D_MODEL ** -0.5),
        'lower_bounds': 1.0 + nrm(ks[7], (DEPTH, A_KEY_WIDTH), 0.1),
        'hgrn_norm': 1.0 + nrm(ks[8], (DEPTH, A_DV), 0.02),
        'q_norm': 1.0 + nrm(ks[9], (DEPTH, B_HD), 0.02),
        'k_norm': 1.0 + nrm(ks[10], (DEPTH, B_HD), 0.02),
        'attn_sinks': nrm(ks[11], (DEPTH, B_HEADS), 0.5),
        'rel_bias_table': nrm(ks[12], (N_BUCKETS, B_HEADS), 0.5),
        'w_out': nrm(ks[13], (DEPTH, MIX_WIDTH, D_MODEL), MIX_WIDTH ** -0.5),
        'norm_ffn': 1.0 + nrm(ks[14], (DEPTH, D_MODEL), 0.02),
        'w_gate': nrm(ks[15], (DEPTH, D_MODEL, D_FF), D_MODEL ** -0.5),
        'w_up': nrm(ks[16], (DEPTH, D_MODEL, D_FF), D_MODEL ** -0.5),
        'w_down': nrm(ks[17], (DEPTH, D_FF, D_MODEL), D_FF ** -0.5),
    }

def reference(x_prompt, x_sample, cache_k, cache_v, state_hgrn, norm_mix, w_in, lower_bounds,
              hgrn_norm, q_norm, k_norm, attn_sinks, rel_bias_table, w_out, norm_ffn,
              w_gate, w_up, w_down):
    p_lb = jax.nn.softmax(lower_bounds.astype(jnp.float32), axis=0)
    lb_all = jnp.cumsum(p_lb, axis=0) - p_lb[0:1]

    bp, seq = x_prompt.shape[0], x_prompt.shape[1]
    nb = seq // WINDOW
    dist_p = (WINDOW + np.arange(WINDOW))[:, None] - np.arange(2 * WINDOW)[None, :]
    key_pos = np.arange(nb)[:, None, None] * WINDOW - WINDOW + np.arange(2 * WINDOW)[None, None, :]
    mask_p = jnp.asarray(((dist_p >= 0) & (dist_p < WINDOW))[None] & (key_pos >= 0))
    bias_p = relative_bias(rel_bias_table, dist_p)
    wp = min(WINDOW, seq)

    bd, ld = x_sample.shape[0], x_sample.shape[1]
    wd = cache_k.shape[2]
    dist_s = (wd + np.arange(ld))[:, None] - np.arange(wd + ld)[None, :]
    mask_s = jnp.asarray((dist_s >= 0) & (dist_s < WINDOW))
    bias_s = relative_bias(rel_bias_table, dist_s)

    xp, xs = x_prompt, x_sample
    pk, pv, ps, sk, sv, ss = [], [], [], [], [], []
    for l in range(DEPTH):
        lb = lb_all[l]
        (qa, lf, ka, va, ga), (qb, kb, vb) = mixer_inputs(xp, norm_mix[l], w_in[l], lb, q_norm[l], k_norm[l])
        oa, st_p = hgrn2_scan(qa, lf, ka, va, jnp.zeros((bp, A_HEADS, A_DK, A_DV), jnp.float32))
        oa = hgrn2_output(oa, hgrn_norm[l], ga, xp.dtype)
        ob = swa_prompt(qb, kb, vb, attn_sinks[l], bias_p, mask_p)
        xp = xp + jnp.concatenate([oa, ob.astype(xp.dtype)], axis=-1) @ w_out[l]
        xp = swiglu(xp, norm_ffn[l], w_gate[l], w_up[l], w_down[l])
        pk.append(kb[:, -wp:])
        pv.append(vb[:, -wp:])
        ps.append(st_p)
        (qa, lf, ka, va, ga), (qb, kb, vb) = mixer_inputs(xs, norm_mix[l], w_in[l], lb, q_norm[l], k_norm[l])
        oa, st_s = hgrn2_scan(qa, lf, ka, va, state_hgrn[l].astype(jnp.float32))
        oa = hgrn2_output(oa, hgrn_norm[l], ga, xs.dtype)
        ob, nk, nv = swa_sample(qb, kb, vb, cache_k[l], cache_v[l], attn_sinks[l], bias_s, mask_s)
        xs = xs + jnp.concatenate([oa, ob.astype(xs.dtype)], axis=-1) @ w_out[l]
        xs = swiglu(xs, norm_ffn[l], w_gate[l], w_up[l], w_down[l])
        sk.append(nk)
        sv.append(nv)
        ss.append(st_s)

    prompt_k, prompt_v, prompt_state = jnp.stack(pk), jnp.stack(pv), jnp.stack(ps)
    sample_k, sample_v, sample_state = jnp.stack(sk), jnp.stack(sv), jnp.stack(ss)
    return (xp, xs, prompt_k, prompt_v, prompt_state, sample_k, sample_v, sample_state)


_drawn_inputs = setup_inputs


def setup_inputs(seed=0):
    import zlib

    import numpy as np

    out = dict(_drawn_inputs(seed))
    spreads = {}
    factors = {'hgrn_norm': 6.212, 'q_norm': 26.227, 'attn_sinks': 82.73, 'norm_ffn': 4.018}
    for name, (base, spread) in spreads.items():
        noise = np.random.default_rng([zlib.crc32(name.encode()), seed]).standard_normal(out[name].shape)
        drawn = base * np.exp(spread * noise) if base else spread * noise
        out[name] = __import__('jax').numpy.asarray(drawn.astype(out[name].dtype))
    for name, factor in factors.items():
        out[name] = (out[name] * factor).astype(out[name].dtype)
    return out
```

```python
import math
from contextlib import ExitStack

import numpy as np

import concourse.bass as bass
from concourse import mybir

F32 = mybir.dt.float32
F32R = mybir.dt.float32r
U8 = mybir.dt.uint8
ALU = mybir.AluOpType
ACT = mybir.ActivationFunctionType
AX = mybir.AxisListType

P = 128
D = 2048
KD = D // P
TP = 256
NB, LB = 8, 4
TS = NB * LB
T = TP + TS
NTT = 3
AH = 8
BH, KVH, G, HD = 16, 4, 4, 64
WIN = 128
F = 5632
EPS = 1e-6
SCALE = 1.0 / math.sqrt(HD)
NEG = -1e30
LB_FLOOR = 1e-20
N_BUCKETS, MAX_DISTANCE = 32, 128

B_Q, B_K, B_V = 8, 2, 2
COL0 = 4096
IN_COLS = ([COL0 + P * i for i in range(12)] + [1024 + P * i for i in range(8)] + [P * i for i in range(8)]
           + [2048 + P * i for i in range(8)] + [3072 + P * i for i in range(8)])
S_F, S_Q, S_I, S_G, S_O, S_O2, S_FFN = 12, 20, 28, 36, 44, 52, 60
FC = 4
NCH = F // (FC * P)
GU, DN = 2 * FC, 4
N_SLABS = S_FFN + NCH * (GU + DN)
RAW, WH, WL = 3, 3, 2
SLAB = 2048
U_O = 44
U_FFN = U_O + 32

S_LUT = 4
S_QKN = 12
S_AT = 14
S_SA = 24
S_LV = 29
S_VT = 30
S_SM = 32
S_PO = 40
S_PS = 41
S_HN = 45
TOKEN_OUTS = 4 + 2 * NB
LEVELS = [0, 1, 2, 4, 8, 16, 32, 64]


def t5_bucket(dist):
    n = np.maximum(dist, 0)
    max_exact = N_BUCKETS // 2
    nf = np.maximum(n, 1).astype(np.float32)
    large = max_exact + (np.log(nf / max_exact) / math.log(MAX_DISTANCE / max_exact)
                         * (N_BUCKETS - max_exact)).astype(np.int32)
    return np.where(n < max_exact, n, np.minimum(large, N_BUCKETS - 1)).astype(np.int32)


def constants():
    ident = np.eye(P, dtype=np.float32)
    pair_win = np.zeros((P, 64), np.float32)
    pair_win[np.arange(P), 32 + np.arange(P) // HD] = 1
    whole_win = np.zeros((P, 64), np.float32)
    whole_win[:, 32:34] = 1
    own = np.zeros((P, NB), np.float32)
    own[np.arange(TS), np.arange(TS) // LB] = 1
    small = np.concatenate([ident, pair_win, whole_win, own], axis=1)
    s, t = np.meshgrid(np.arange(P), np.arange(P), indexing="ij")
    masks = np.stack([(s == t) if lv == 0 else
                      ((s // (2 * lv) == t // (2 * lv)) & (s // lv % 2 == 0) & (t // lv % 2 == 1))
                      for lv in LEVELS], axis=1).astype(np.float32).reshape(P, -1)
    dist = 255 - np.arange(384)
    ok = (dist >= 0) & (dist < WIN)
    row = np.where(ok, t5_bucket(dist), N_BUCKETS)
    bucket_of = (np.arange(33)[:, None] == row[None]).astype(np.float32)
    rows_of = np.zeros((BH, LB, P), np.float32)
    for h in range(BH):
        for l in range(LB):
            rows_of[h, l, 32 * (h // G) + LB * (h % G) + l] = 1
    early = np.zeros((P, 384 + LB * P), np.float32)
    early[0:33, 0:384] = bucket_of
    early[0:BH, 384:] = rows_of.reshape(BH, -1)
    return small, masks, early


def layer_kernel(nc, x_prompt, x_sample, cache_k, cache_v, state_hgrn, norm_mix, w_in, lower_bounds, hgrn_norm,
                 q_norm, k_norm, attn_sinks, rel_bias_table, w_out, norm_ffn, w_gate, w_up, w_down,
                 c_small, c_masks, c_early,
                 y_prompt, y_sample, prompt_k, prompt_v, prompt_state, sample_k, sample_v, sample_state):
    w_in, w_out, w_gate, w_up, w_down = w_in[0], w_out[0], w_gate[0], w_up[0], w_down[0]
    win_v = w_in.rearrange("(k p) c -> p k c", p=P)
    wout_v = w_out.rearrange("(k p) c -> p k c", p=P)
    wg_v = w_gate.rearrange("(k p) c -> p k c", p=P)
    wu_v = w_up.rearrange("(k p) c -> p k c", p=P)
    x_spill = nc.dram_tensor("x_spill", (P, KD * T), F32).ap()
    bias_rows = nc.dram_tensor("bias_rows", (BH, P, 384), F32).ap()

    with ExitStack() as ctx:
        def sb(name, shape, dt=F32):
            return ctx.enter_context(nc.sbuf_tensor(name, shape, dt))

        def sem(name):
            return ctx.enter_context(nc.semaphore(name))

        raw = sb("raw", [P, RAW, SLAB])
        wh = sb("wh", [P, WH, SLAB], F32R)
        wl = sb("wl", [P, WL, SLAB], F32R)
        act_h = sb("act_h", [P, KD, T], F32R)
        act_l = sb("act_l", [P, KD, T], F32R)
        mix_h = sb("mix_h", [P, 8, T], F32R)
        mix_l = sb("mix_l", [P, 8, T], F32R)
        reg_x = sb("reg_x", [P, KD * T])
        reg_qkf = sb("reg_qkf", [P, 3 * 8 * T])
        reg_g = sb("reg_g", [P, 8, T])
        reg_v = sb("reg_v", [P, 3072])
        reg_a = sb("reg_a", [P, 3072])
        reg_t = sb("reg_t", [P, 2016])
        small = sb("small", [P, 264])
        masks = sb("masks", [P, len(LEVELS) * P], U8)
        gains = sb("gains", [P, 2, KD])
        head_g = sb("head_g", [P, 4])
        sinks = sb("sinks", [P, BH])
        lbs = sb("lbs", [P, 4, AH])
        st = sb("st", [P, 2, 5, 4])
        ones = sb("ones", [P, P])
        ident = small[:, 0:128]
        pair_win = small[:, 128:192]
        whole_win = small[:, 192:256]
        own = small[0:TS, 256:264]

        xT = reg_x[:, :].rearrange("p (k t) -> p k t", k=KD)
        xtok = reg_qkf[:, 0:NTT * D].rearrange("p (j d) -> p j d", j=NTT)
        q_a = reg_qkf[:, 0:8 * T].rearrange("p (h t) -> p h t", h=AH)
        k_a = reg_qkf[:, 8 * T:16 * T].rearrange("p (h t) -> p h t", h=AH)
        f_a = reg_qkf[:, 16 * T:24 * T].rearrange("p (h t) -> p h t", h=AH)
        tmp = reg_t[:, :].rearrange("p (n t) -> p n t", t=T)
        kvT = reg_v[:, 0:1152].rearrange("p (c t) -> p c t", c=4)
        k_both = reg_v[:, 1152:2304].rearrange("p (k t) -> p k t", k=KVH)
        v_tok = reg_v[:, 2304:3072].rearrange("p (j c) -> p j c", j=NTT)
        scores = reg_a[:, 0:2048].rearrange("p (n h s) -> p n h s", n=2, h=G)
        bias_buf = [reg_a[:, 2048:3072].rearrange("p (h s) -> p h s", h=G),
                    reg_x[:, 0:1024].rearrange("p (h s) -> p h s", h=G)]
        probs_t = reg_x[:, 1024:2048].rearrange("p (b h t) -> p b h t", b=2, h=G)
        v_cache = reg_x[:, 2048:4096].rearrange("p (b c) -> p b c", b=NB)
        k_tok = reg_x[:, 4096:4608].rearrange("p (j c) -> p j c", j=2)
        NK = WIN + TS
        s_scores = reg_a[:, 0:NB * NK].rearrange("p (b s) -> p b s", b=NB)
        s_bias_new = reg_a[:, 1280:1536].rearrange("p (b s) -> p b s", b=NB)
        k_cache = [reg_a[:, 1536:2048].rearrange("p (n c) -> p n c", n=2),
                   reg_t[:, 576:1088].rearrange("p (n c) -> p n c", n=2)]
        q_rows = reg_a[:, 2048:3072].rearrange("p (k b m) -> p k b m", k=KVH, b=NB)
        kT_cache = reg_x[:, 0:4 * NK].rearrange("p (n c s) -> p n c s", n=2, c=2)
        s_probs_t = reg_x[:, 1024:2048].rearrange("p (b m) -> p b m", b=NB)
        s_new_t = reg_t[0:TS, 576:1600].rearrange("p (b m) -> p b m", b=NB)
        s_out = reg_x[:, 640:896].rearrange("p (m t) -> p m t", m=8)
        s_bias = reg_t[:, 1600:1732]
        s_st = reg_t[:, 1732:1772].rearrange("p (n b) -> p n b", n=5)
        norm_rows = reg_t[0:32, 1152:1440]
        head_rows = reg_qkf[0:32, 0:20 * HD]
        early = reg_a[:, 0:896]
        table = reg_a[0:33, 896:912]
        by_dist = reg_a[0:BH, 912:1296]
        sink_col = reg_a[0:BH, 1296:1297]
        masks_f = reg_v[:, 0:len(LEVELS) * P]
        v_a = reg_v[:, :].rearrange("p (j c) -> p j c", j=NTT)
        a_t = reg_a[:, :].rearrange("p (h n t) -> p h n t", h=AH, n=3)
        a_s = reg_t[0:TS, 1152:1408].rearrange("p (h t) -> p h t", h=AH)
        iT = tmp[:, 2:4, :]
        sig = tmp[:, 0:2, :]
        s0 = reg_x[:, 0:2048].rearrange("p (n b v) -> p n b v", n=2, b=NB)
        v_own = reg_x[0:TS, 2048:4096].rearrange("p (n b v) -> p n b v", n=2, b=NB)
        kt_s = reg_x[0:TS, 4096:4352].rearrange("p (n k) -> p n k", n=2)
        kt_p = reg_t[:, 1408:1920].rearrange("p (n j k) -> p n j k", n=2, j=2)
        st_p = reg_t[:, 576:832].rearrange("p (n v) -> p n v", n=2)
        h_rows = reg_t[0:32, 1408:1696]
        rstd2 = tmp[:, 6, :]

        acc = [ctx.enter_context(nc.psum_tensor(f"acc{i}", [P, 512], F32)) for i in range(4)]
        mx = ctx.enter_context(nc.psum_tensor("mx", [P, 4, 512], F32))

        x_in = sem("x_in")
        consts_in = sem("consts_in")
        small_in = sem("small_in")
        early_in = sem("early_in")
        raw_in = [sem(f"raw_in{i}") for i in range(RAW)]
        high_done = sem("high_done")
        low_done = sem("low_done")
        unit_done = sem("unit_done")
        ones_set = sem("ones_set")
        dve_seq = sem("dve_seq")
        act_seq = sem("act_seq")
        xt_done = sem("xt_done")
        xt_copied = sem("xt_copied")
        sq_done = sem("sq_done")
        ssq_done = sem("ssq_done")
        ms_done = sem("ms_done")
        rt_done = sem("rt_done")
        xn_done = sem("xn_done")
        acth_done = sem("acth_done")
        actl_done = sem("actl_done")
        spilled = sem("spilled")
        reloaded = sem("reloaded")
        qkv_done = sem("qkv_done")
        qk_sq = sem("qk_sq")
        qk_ssq = sem("qk_ssq")
        rows_spread = sem("rows_spread")
        rows_done = sem("rows_done")
        qk_bc = sem("qk_bc")
        qk_normed = sem("qk_normed")
        k_copied = sem("k_copied")
        vk_t = sem("vk_t")
        vk_tok = sem("vk_tok")
        lut_done = sem("lut_done")
        lut_copied = sem("lut_copied")
        masks_done = sem("masks_done")
        lut_out = sem("lut_out")
        bias_in = [sem("bias_in0"), sem("bias_in1")]
        sc_done = sem("sc_done")
        sc_biased = sem("sc_biased")
        sc_max = sem("sc_max")
        sc_exp = sem("sc_exp")
        sc_inv = sem("sc_inv")
        sc_probs = sem("sc_probs")
        pt_done = sem("pt_done")
        pt_copied = sem("pt_copied")
        pv_done = sem("pv_done")
        mixh_done = sem("mixh_done")
        mixl_done = sem("mixl_done")
        vc_in = sem("vc_in")
        kc_in = [sem("kc_in0"), sem("kc_in1")]
        kc_t = sem("kc_t")
        kc_copied = sem("kc_copied")
        kn_copied = sem("kn_copied")
        qr_zero = sem("qr_zero")
        sb_new = sem("sb_new")
        qr_done = sem("qr_done")
        ss_done = sem("ss_done")
        ss_biased = sem("ss_biased")
        ss_max = sem("ss_max")
        ss_exp = sem("ss_exp")
        ss_probs = sem("ss_probs")
        sp_t = sem("sp_t")
        sp_copied = sem("sp_copied")
        so_done = sem("so_done")
        so_copied = sem("so_copied")
        lb_sub = sem("lb_sub")
        lb_exp = sem("lb_exp")
        lb_done = sem("lb_done")
        f_sig = sem("f_sig")
        k_made = sem("k_made")
        q_sig = sem("q_sig")
        q_made = sem("q_made")
        i_copied = sem("i_copied")
        g_sig = sem("g_sig")
        g_made = sem("g_made")
        v_t = sem("v_t")
        v_tokd = sem("v_tokd")
        lv_done = sem("lv_done")
        lv_kept = sem("lv_kept")
        lv_next = sem("lv_next")
        at_zero = sem("at_zero")
        s0_in = [sem("s0_in0"), sem("s0_in1")]
        kt_copied = sem("kt_copied")
        v_owned = sem("v_owned")
        sm_o = sem("sm_o")
        sm_oc = sem("sm_oc")
        sm_st = sem("sm_st")
        s0_new = sem("s0_new")
        s0_out = [sem("s0_out0"), sem("s0_out1")]
        po_done = sem("po_done")
        po_copied = sem("po_copied")
        ktp_done = sem("ktp_done")
        ktp_copied = sem("ktp_copied")
        ps_done = sem("ps_done")
        ps_copied = sem("ps_copied")
        ps_out = sem("ps_out")
        h_sq = sem("h_sq")
        h_ssq = sem("h_ssq")
        h_rowsd = sem("h_rowsd")
        h_bc = sem("h_bc")
        h_normed = sem("h_normed")
        h_gated = sem("h_gated")
        hh_done = sem("hh_done")
        hl_done = sem("hl_done")
        x_added = sem("x_added")
        sq2_done = sem("sq2_done")
        ssq2_done = sem("ssq2_done")
        xg_done = sem("xg_done")
        xgh_done = sem("xgh_done")
        xgl_done = sem("xgl_done")
        rstd2_done = sem("rstd2_done")
        gate_scaled = sem("gate_scaled")
        gate_silu = sem("gate_silu")
        gate_ready = sem("gate_ready")
        inner_done = sem("inner_done")
        innerh_done = sem("innerh_done")
        innerl_done = sem("innerl_done")
        down_added = sem("down_added")
        yt_done = sem("yt_done")
        yt_copied_a = sem("yt_copied_a")
        yt_copied_v = sem("yt_copied_v")
        y_out = sem("y_out")
        outs = sem("outs")
        n_outs = [0]

        def out_dma(eng, dst, src):
            eng.dma_start(dst, src).then_inc(outs, 16)
            n_outs[0] += 1

        block = ctx.enter_context(nc.Block())

        def units_through(s):
            return s + 1 if s < S_O else U_O + 2 * (s - S_O + 1)

        def units_ffn(c, i, down):
            if down:
                return U_FFN + 8 * (c + 2 if isinstance(c, int) and c < NCH - 1 or not isinstance(c, int) else NCH) \
                    + 16 * c + 4 * (i + 1)
            if isinstance(c, int) and c < 2:
                return U_FFN + 8 * c + i + 1
            return U_FFN + 8 * c + 16 * (c - 1) + i + 1

        def gu_slab(c):
            return S_FFN + 8 * c if isinstance(c, int) and c < 2 else S_FFN + 8 * c + 4 * (c - 1)

        def dn_slab(c):
            return S_FFN + 8 * NCH + 4 * c if isinstance(c, int) and c == NCH - 1 else S_FFN + 8 * (c + 2) + 4 * c

        def ffn_walk(eng, gate_up, down):
            gate_up(0, 0)
            gate_up(1, 1)
            down(0, 0)
            with eng.Fori(0, (NCH - 3) // 2) as j:
                gate_up(2 * j + 2, 2)
                down(2 * j + 1, 1)
                gate_up(2 * j + 3, 3)
                down(2 * j + 2, 2)
            gate_up(NCH - 1, NCH - 1)
            down(NCH - 2, NCH - 2)
            down(NCH - 1, NCH - 1)

        @block.sync
        def _(sp):
            for j in range(2):
                sp.dma_start(xtok[:, j, :], x_prompt[0, P * j:P * j + P, :]).then_inc(x_in, 16)
            sp.dma_start(xtok[0:TS, 2, :], x_sample.rearrange("b l d -> (b l) d")).then_inc(x_in, 16)

            def load(s, slot, src, k):
                if not (isinstance(s, int) and s < RAW):
                    sp.wait_ge(low_done, s - RAW + 1)
                sp.dma_start(raw[:, slot % RAW, :].rearrange("p (k c) -> p k c", k=k), src)\
                    .then_inc(raw_in[slot % RAW], 16)

            for s in range(S_O):
                load(s, s, win_v[:, :, IN_COLS[s]:IN_COLS[s] + P], KD)
            for s in range(S_O, S_FFN):
                half, m = divmod(s - S_O, 8)
                rows = slice(8, 16) if half == 0 else slice(0, 8)
                load(s, s, wout_v[:, rows, 2 * P * m:2 * P * (m + 1)], 8)

            def gate_up(c, cs):
                for i in range(GU):
                    src = (wg_v if i % 2 == 0 else wu_v)[:, :, bass.ds(c * (FC * P) + P * (i // 2), P)]
                    load(gu_slab(c) + i, gu_slab(cs) + i, src, KD)

            def down(c, cs):
                for i in range(DN):
                    src = w_down[bass.ds(c * (FC * P), FC * P), 512 * i:512 * i + 512]\
                        .rearrange("(k p) n -> p k n", p=P)
                    load(dn_slab(c) + i, dn_slab(cs) + i, src, FC)

            ffn_walk(sp, gate_up, down)
            for q in range(4):
                cols = slice(512 * q, 512 * q + 512)
                sp.wait_ge(yt_copied_a, 2 * q + 2)
                sp.wait_ge(yt_copied_v, q + 1)
                for j in range(2):
                    sp.dma_start(y_prompt[0, P * j:P * j + P, cols], xtok[:, j, cols]).then_inc(y_out, 16)
                sp.dma_start(y_sample.rearrange("b l d -> (b l) d")[:, cols], xtok[0:TS, 2, cols]).then_inc(y_out, 16)
            sp.wait_ge(y_out, 16 * 12)

        @block.gpsimd
        def _(pool):
            nc.gpsimd.memset(ones[:], 1.0).then_inc(ones_set, 1)
            pool.dma_start(masks_f, c_masks).then_inc(early_in, 16)
            with nc.allow_non_contiguous_dma(reason="gains, a few KB"):
                pool.dma_start(gains[:, 0, :], norm_mix.rearrange("o (k p) -> p (o k)", p=P)).then_inc(consts_in, 16)
                pool.dma_start(gains[:, 1, :], norm_ffn.rearrange("o (k p) -> p (o k)", p=P)).then_inc(consts_in, 16)
                for half in range(2):
                    rows = slice(HD * half, HD * half + HD)
                    pool.dma_start(head_g[rows, 0:1], q_norm.rearrange("o d -> d o")).then_inc(consts_in, 16)
                    pool.dma_start(head_g[rows, 1:2], k_norm.rearrange("o d -> d o")).then_inc(consts_in, 16)
                pool.dma_start(head_g[:, 2:3], hgrn_norm.rearrange("o d -> d o")).then_inc(consts_in, 16)
                pool.dma_start(lbs[:, 0, :], lower_bounds.rearrange("o (h p) -> p (o h)", p=P)).then_inc(consts_in, 16)
                pool.dma_start(sinks[:, :], bass.AP(attn_sinks.tensor, 0, [[0, P], [1, BH]])).then_inc(consts_in, 16)
                pool.dma_start(early, c_early).then_inc(early_in, 16)
                pool.dma_start(table[0:N_BUCKETS, :], rel_bias_table).then_inc(early_in, 16)
                pool.dma_start(sink_col, attn_sinks.rearrange("o h -> h o")).then_inc(early_in, 16)
            pool.wait_ge(ones_set, 1)
            nc.gpsimd.memset(table[32:33, :], NEG).then_inc(at_zero, 1)
            pool.wait_ge(at_zero, 1)
            pool.wait_ge(xt_copied, KD)
            pool.dma_start(x_spill, reg_x[:, :]).then_inc(spilled, 16)
            pool.wait_ge(small_in, 16)
            nc.gpsimd.tensor_copy(head_rows.rearrange("p (c d) -> p c d", d=HD),
                                  ident[0:32, 0:20].unsqueeze(2).broadcast_to([32, 20, HD])).then_inc(rows_spread, 1)
            pool.wait_ge(lut_copied, 1)
            for h in range(BH):
                pool.dma_start(bias_rows[h:h + 1], by_dist[h:h + 1, :].unsqueeze(1).broadcast_to([1, P, 384]))\
                    .then_inc(lut_out, 16)
            pool.wait_ge(lut_out, 16 * BH)

            def load_bias(k):
                for par in range(2):
                    for gg in range(2):
                        head = G * k + 2 * gg + par
                        src = bass.AP(bias_rows.tensor, head * P * 384 + 127, [[383, P], [1, 2 * WIN]])
                        pool.dma_start(bias_buf[k % 2][:, 2 * par + gg, :], src).then_inc(bias_in[k % 2], 16)

            load_bias(0)
            pool.wait_ge(spilled, 16)
            load_bias(1)
            pool.dma_start(v_cache[:, :, :], cache_v[0].rearrange("b s k d -> s b (k d)")).then_inc(vc_in, 16)
            out_dma(pool, sample_k[0, :, 0:WIN - LB].rearrange("b s k d -> b (s k d)"),
                    cache_k[0, :, LB:WIN].rearrange("b s k d -> b (s k d)"))
            out_dma(pool, sample_v[0, :, 0:WIN - LB].rearrange("b s k d -> b (s k d)"),
                    cache_v[0, :, LB:WIN].rearrange("b s k d -> b (s k d)"))

            for n in range(2 * KVH):
                k, j = divmod(n, 2)
                pool.wait_ge(sc_exp, n + 1)
                pool.wait_ge(sc_inv, n + 1)
                cols = slice(0, 2 * WIN) if j else slice(WIN, 2 * WIN)
                width = 2 * WIN if j else WIN
                sc = scores[:, n % 2, :, cols]
                nc.gpsimd.tensor_tensor(sc, sc, st[:, n % 2, 4, :].unsqueeze(2).broadcast_to([P, G, width]),
                                        ALU.mult).then_inc(sc_probs, 1)
                if j == 1 and k + 2 < KVH:
                    pool.wait_ge(sc_biased, n + 1)
                    load_bias(k + 2)
                if n == 1:
                    pool.wait_ge(vk_tok, 3)
                    out_dma(pool, prompt_k[0, 0].rearrange("s k d -> s (k d)"), k_tok[:, 0, :])
                    out_dma(pool, prompt_v[0, 0].rearrange("s k d -> s (k d)"), v_tok[:, 1, :])
                    for b in range(NB):
                        rows = slice(LB * b, LB * b + LB)
                        out_dma(pool, sample_k[0, b, WIN - LB:WIN].rearrange("s k d -> s (k d)"), k_tok[rows, 1, :])
                        out_dma(pool, sample_v[0, b, WIN - LB:WIN].rearrange("s k d -> s (k d)"), v_tok[rows, 2, :])
            pool.wait_ge(sc_biased, 2 * KVH)
            pool.wait_ge(pt_done, 2 * KVH)
            nc.gpsimd.memset(q_rows, 0.0).then_inc(qr_zero, 1)
            nc.gpsimd.memset(s_bias_new, NEG).then_inc(qr_zero, 1)
            for i in range(NB // 2):
                if i >= 2:
                    pool.wait_ge(kc_t, i - 1)
                for n in range(2):
                    pool.dma_start(k_cache[i % 2][:, n, :], cache_k[0, 2 * i + n].rearrange("s k d -> s (k d)"))\
                        .then_inc(kc_in[i % 2], 16)
            pool.wait_ge(so_copied, 2)
            nc.gpsimd.memset(reg_a[:, :], 0.0).then_inc(at_zero, 1)
            nc.gpsimd.memset(a_s, 0.0).then_inc(at_zero, 1)

            def load_state(h):
                pool.dma_start(s0[:, h % 2], state_hgrn[0, :, h].rearrange("b k v -> k b v")).then_inc(s0_in[h % 2], 16)

            pool.wait_ge(mixl_done, 2 * KVH + 1)
            pool.wait_ge(outs, 16 * TOKEN_OUTS)
            load_state(0)
            load_state(1)
            for h in range(AH):
                pool.wait_ge(v_tokd, h + 1)
                if h >= 2:
                    pool.wait_ge(sm_st, 2 * (h - 1))
                nc.gpsimd.tensor_tensor(
                    v_own[:, h % 2], v_a[0:TS, 2, P * h:P * h + P].unsqueeze(1).broadcast_to([TS, NB, P]),
                    own.unsqueeze(2).broadcast_to([TS, NB, P]), ALU.mult).then_inc(v_owned, 1)
                if h >= 1:
                    pool.wait_ge(s0_new, 2 * h)
                    pool.dma_start(sample_state[0, :, h - 1].rearrange("b k v -> k b v"), s0[:, (h - 1) % 2])\
                        .then_inc(s0_out[(h - 1) % 2], 16)
                    if h + 1 < AH:
                        pool.wait_ge(s0_out[(h - 1) % 2], 16 * ((h - 1) // 2 + 1))
                        load_state(h + 1)
            pool.wait_ge(s0_new, 2 * AH)
            pool.dma_start(sample_state[0, :, AH - 1].rearrange("b k v -> k b v"), s0[:, (AH - 1) % 2])\
                .then_inc(s0_out[(AH - 1) % 2], 16)
            for n in range(2):
                pool.wait_ge(s0_out[n], 16 * AH // 2)
            pool.dma_start(reg_x[:, :], x_spill).then_inc(reloaded, 16)
            for i in range(AH // 2):
                pool.wait_ge(ps_copied, i + 1)
                pool.dma_start(prompt_state[0, 0, 2 * i:2 * i + 2].rearrange("h k v -> k h v"), st_p)\
                    .then_inc(ps_out, 16)
            pool.wait_ge(ps_out, 16 * AH // 2)
            pool.wait_ge(h_ssq, AH)
            for m in range(KD):
                pool.wait_ge(x_added, 17 + m)
                if m >= 2:
                    pool.wait_ge(sq2_done, 2 * m - 1)
                nc.gpsimd.tensor_tensor(tmp[:, 1 if m else 0, :], xT[:, m, :], xT[:, m, :], ALU.mult)\
                    .then_inc(sq2_done, 1)
                if m:
                    pool.wait_ge(sq2_done, 2 * m)
                    nc.gpsimd.tensor_tensor(tmp[:, 0, :], tmp[:, 0, :], tmp[:, 1, :], ALU.add).then_inc(sq2_done, 1)
            pool.wait_ge(outs, 16 * n_outs[0])

        @block.scalar
        def _(act):
            seq = [0]

            def link(ins):
                seq[0] += 1
                ins.then_inc(act_seq, 1)
                act.wait_ge(act_seq, seq[0])

            def high(s, slot, units):
                act.wait_ge(raw_in[slot % RAW], 16 * ((s - slot % RAW) // RAW + 1) if isinstance(s, int) else
                            raw_count(s, slot))
                if units is not None:
                    act.wait_ge(unit_done, units)
                nc.scalar.activation(wh[:, slot % WH, :], raw[:, slot % RAW, :], ACT.Copy).then_inc(high_done, 1)

            def x_tiles():
                for k in range(KD):
                    act.wait_ge(xt_done, k + 1)
                    nc.scalar.activation(xT[:, k, :], mx[:, k % 4, 0:T], ACT.Copy).then_inc(xt_copied, 1)
                    if k >= 2:
                        act.wait_ge(ssq_done, k - 1)
                    nc.scalar.activation(tmp[:, k % 2, :], mx[:, k % 4, 0:T], ACT.Square).then_inc(sq_done, 1)

            def root(n, rows):
                act.wait_ge(ms_done, n)
                nc.scalar.activation(rows, rows, ACT.Sqrt).then_inc(rt_done, 1)

            def x_high():
                for k in range(KD):
                    act.wait_ge(xn_done, k + 1)
                    nc.scalar.activation(act_h[:, k, :], tmp[:, 2 + k % 4, :], ACT.Copy).then_inc(acth_done, 1)

            def lower_bound():
                act.wait_ge(lb_sub, 1)
                nc.scalar.activation(lbs[:, 2, :], lbs[:, 1, :], ACT.Exp).then_inc(lb_exp, 1)

            def evacuate(s):
                act.wait_ge(unit_done, s + 1)
                ps = acc[s % 4][:, 0:T]
                if s < S_F:
                    if s < 8:
                        dst = reg_g[:, s, :]
                    else:
                        act.wait_ge(masks_done, 1)
                        dst = kvT[:, s - 8, :]
                    if s < 10:
                        if s >= 2:
                            act.wait_ge(qk_ssq, s - 1)
                        nc.scalar.activation(tmp[:, s % 2, :], ps, ACT.Square).then_inc(qk_sq, 1)
                    nc.scalar.activation(dst, ps, ACT.Copy).then_inc(qkv_done, 1)
                elif s < S_Q:
                    h = s - S_F
                    nc.scalar.activation(f_a[:, h, :], ps, ACT.Sigmoid)
                    nc.scalar.activation(k_a[:, h, :], ps, ACT.Sigmoid, scale=-1.0).then_inc(f_sig, 1)
                elif s < S_I:
                    h = s - S_Q
                    if h >= 2:
                        act.wait_ge(q_made, h - 1)
                    nc.scalar.activation(sig[:, h % 2, :], ps, ACT.Sigmoid).then_inc(q_sig, 1)
                elif s < S_G:
                    h = s - S_I
                    if h == 0:
                        act.wait_ge(so_done, 1)
                    if h >= 2:
                        act.wait_ge(v_t, h - 1)
                    nc.scalar.activation(iT[:, h % 2, :], ps, ACT.Copy).then_inc(i_copied, 1)
                elif s < S_O:
                    h = s - S_G
                    if h >= 2:
                        act.wait_ge(g_made, h - 1)
                    nc.scalar.activation(sig[:, h % 2, :], ps, ACT.Sigmoid).then_inc(g_sig, 1)

            def k_halves():
                act.wait_ge(qk_normed, 10)
                for k in range(KVH):
                    src = kvT[HD * (k % 2):HD * (k % 2) + HD, k // 2, :]
                    for half in range(2):
                        nc.scalar.activation(k_both[HD * half:HD * half + HD, k, :], src, ACT.Copy)\
                            .then_inc(k_copied, 1)

            def token_major():
                act.wait_ge(vk_t, 1)
                nc.scalar.activation(v_tok[:, 0:2, :], mx[:, 0, :].rearrange("p (j c) -> p j c", j=2), ACT.Copy)\
                    .then_inc(vk_tok, 1)
                act.wait_ge(vk_t, 2)
                act.wait_ge(spilled, 16)
                nc.scalar.activation(k_tok[:, 0, :], mx[:, 2, 0:256], ACT.Copy)
                nc.scalar.activation(v_tok[0:TS, 2, :], mx[0:TS, 1, 0:256], ACT.Copy).then_inc(vk_tok, 1)
                nc.scalar.activation(k_tok[0:TS, 1, :], mx[0:TS, 1, 256:512], ACT.Copy).then_inc(vk_tok, 1)

            def exps(n):
                j = n % 2
                cols = slice(0, 2 * WIN) if j else slice(WIN, 2 * WIN)
                act.wait_ge(sc_max, n + 1)
                nc.scalar.activation(st[:, n % 2, 2, :], st[:, n % 2, 2, :], ACT.Exp)
                for h in range(G):
                    sc = scores[:, n % 2, h, cols]
                    ins = nc.scalar.activation(sc, sc, ACT.Exp, bias=st[:, n % 2, 1, h:h + 1],
                                               accum_out=st[:, n % 2, 3, h:h + 1])
                ins.then_inc(sc_exp, 1)

            def probs_copy(n):
                j = n % 2
                act.wait_ge(pt_done, n + 1)
                if n >= 1:
                    act.wait_ge(pv_done, n)
                for blk in range(1 - j, 2):
                    ins = nc.scalar.activation(probs_t[:, blk], mx[:, 2 + blk, :].rearrange("p (h t) -> p h t", h=G),
                                               ACT.Copy)
                ins.then_inc(pt_copied, 1)

            def out_high(n):
                k, j = divmod(n, 2)
                act.wait_ge(pv_done, n + 1)
                nc.scalar.activation(mix_h[:, 2 * k:2 * k + 2, P * j:P * j + P],
                                     mx[:, 2, 0:256].rearrange("p (m t) -> p m t", m=2), ACT.Copy).then_inc(mixh_done, 1)

            def q_to_rows():
                act.wait_ge(qr_zero, 2)
                for k in range(KVH):
                    for g in range(G):
                        src = reg_g[HD * (g % 2):HD * (g % 2) + HD, 2 * k + g // 2, TP:T]
                        dst = q_rows[HD * (k % 2):HD * (k % 2) + HD, k, :, LB * g:LB * g + LB]
                        nc.scalar.activation(dst, src.rearrange("p (b l) -> p b l", b=NB), ACT.Copy)\
                            .then_inc(qr_done, 1)
                act.wait_ge(sc_biased, 2 * KVH)
                for n in range(2):
                    nc.scalar.activation(kT_cache[:, n, :, WIN:NK], kvT[:, 0:2, TP:T], ACT.Copy).then_inc(kn_copied, 1)

            def s_exps():
                act.wait_ge(ss_max, 1)
                nc.scalar.activation(s_st[:, 2, :], s_st[:, 2, :], ACT.Exp)
                for b in range(NB):
                    ins = nc.scalar.activation(s_scores[:, b, :], s_scores[:, b, :], ACT.Exp,
                                               bias=s_st[:, 1, b:b + 1], accum_out=s_st[:, 3, b:b + 1])
                ins.then_inc(ss_exp, 1)

            def s_probs_copy(n):
                act.wait_ge(sp_t, n + 1)
                nc.scalar.activation(s_probs_t[:, 4 * n:4 * n + 4, :],
                                     mx[:, 2 * n, :].rearrange("p (b m) -> p b m", b=4), ACT.Copy)
                nc.scalar.activation(s_new_t[:, 4 * n:4 * n + 4, :],
                                     mx[0:TS, 2 * n + 1, :].rearrange("p (b m) -> p b m", b=4), ACT.Copy)\
                    .then_inc(sp_copied, 1)

            def s_out_copy():
                act.wait_ge(so_done, 1)
                src = mx[0:HD, 0, :].rearrange("p (k b m) -> p k b m", k=KVH, b=NB)
                dst = s_out.rearrange("p (k m) (b l) -> p k m b l", k=KVH, b=NB)
                for g in range(G):
                    ins = nc.scalar.activation(dst[HD * (g % 2):HD * (g % 2) + HD, :, g // 2],
                                               src[:, :, :, LB * g:LB * g + LB], ACT.Copy)
                ins.then_inc(so_copied, 1)
                act.wait_ge(so_copied, 1)
                nc.scalar.activation(mix_h[:, :, TP:T], s_out, ACT.Copy).then_inc(so_copied, 1)

            def v_copy(h):
                if h == 0:
                    act.wait_ge(outs, 16 * TOKEN_OUTS)
                act.wait_ge(v_t, h + 1)
                nc.scalar.activation(v_a[:, 0:2, P * h:P * h + P],
                                     mx[:, 0, 0:256].rearrange("p (j c) -> p j c", j=2), ACT.Copy)
                nc.scalar.activation(v_a[0:TS, 2, P * h:P * h + P], mx[0:TS, 0, 256:384], ACT.Copy)\
                    .then_inc(v_tokd, 1)

            def sampled_copies(h):
                act.wait_ge(sm_o, h + 1)
                if h >= 2:
                    act.wait_ge(sm_st, 2 * (h - 1))
                nc.scalar.activation(kt_s[:, h % 2, :], mx[0:TS, 1, 128:256], ACT.Copy).then_inc(kt_copied, 1)
                nc.scalar.activation(q_a[:, h, TP:T], mx[:, 1, 0:TS], ACT.Copy).then_inc(sm_oc, 1)

            def prompt_out_copy(h):
                act.wait_ge(po_done, h + 1)
                nc.scalar.activation(q_a[:, h, 0:TP], mx[:, h % 2, 0:TP], ACT.Copy).then_inc(po_copied, 1)

            def prompt_state_copies(i):
                act.wait_ge(ktp_done, i + 1)
                nc.scalar.activation(kt_p, mx[:, 2, :].rearrange("p (n j k) -> p n j k", n=2, j=2), ACT.Copy)\
                    .then_inc(ktp_copied, 1)
                act.wait_ge(ps_done, i + 1)
                if i:
                    act.wait_ge(ps_out, 16 * i)
                nc.scalar.activation(st_p, mx[:, 3, 0:256].rearrange("p (n v) -> p n v", n=2), ACT.Copy)\
                    .then_inc(ps_copied, 1)

            def h_squares(heads):
                act.wait_ge(g_made, AH)
                act.wait_ge(po_copied, AH)
                act.wait_ge(sm_oc, AH)
                for h in heads:
                    if h >= 2:
                        act.wait_ge(h_ssq, h - 1)
                    nc.scalar.activation(sig[:, h % 2, :], q_a[:, h, :], ACT.Square).then_inc(h_sq, 1)

            def h_high(heads):
                for h in heads:
                    act.wait_ge(h_gated, h + 1)
                    nc.scalar.activation(act_h[:, h, :], q_a[:, h, :], ACT.Copy).then_inc(hh_done, 1)

            def x2_high(m):
                act.wait_ge(xg_done, m + 1)
                act.wait_ge(unit_done, U_FFN)
                nc.scalar.activation(act_h[:, m, :], tmp[:, 2 + m % 4, :], ACT.Copy).then_inc(xgh_done, 1)

            def raw_count(s, slot):
                return (s - slot % RAW) * 16 // RAW + 16

            act.dma_start(small[:, :], c_small).then_inc(small_in, 16)
            x_tiles()
            root(1, tmp[:, 6, :])
            high(0, 0, None)
            x_high()
            lower_bound()
            high(1, 1, None)
            high(2, 2, None)
            for s in range(S_FFN):
                if 0 <= s - S_AT - 2 < 8:
                    out_high(s - S_AT - 2)
                if 0 <= s - S_AT < 8:
                    exps(s - S_AT)
                if 0 <= s - S_AT - 1 < 8:
                    probs_copy(s - S_AT - 1)
                if s == S_QKN - 1:
                    root(2, norm_rows)
                if s == S_QKN:
                    k_halves()
                    token_major()
                if s == S_SA - 1:
                    q_to_rows()
                if s == S_SA + 2:
                    s_exps()
                if s == S_SA + 3:
                    s_probs_copy(0)
                    s_probs_copy(1)
                if s == S_SA + 4:
                    s_out_copy()
                if 0 <= s - S_PO < 4:
                    prompt_out_copy(2 * (s - S_PO))
                    prompt_out_copy(2 * (s - S_PO) + 1)
                if 0 <= s - S_VT < AH:
                    v_copy(s - S_VT)
                if 0 <= s - S_SM < AH:
                    sampled_copies(s - S_SM)
                if 0 <= s - S_PS < 4:
                    prompt_state_copies(s - S_PS)
                if s == S_HN:
                    h_squares(range(2, 6))
                if s == S_HN + 1:
                    h_squares(range(6, 8))
                    root(3, h_rows)
                if s in (S_HN + 2, S_HN + 3):
                    h_high(range(4 * (s - S_HN - 2), 4 * (s - S_HN - 1)))
                if s < S_O:
                    evacuate(s)
                if s == S_HN - 1:
                    h_squares(range(0, 2))
                if s + WH < S_FFN + GU:
                    high(s + WH, s + WH, units_through(s))
            for m in range(KD):
                x2_high(m)
            root(4, rstd2)

            def gate_up(c, cs):
                for i in range(GU):
                    t, up = divmod(i, 2)
                    n = c * FC + t
                    if not up:
                        act.wait_ge(gate_scaled, n + 1)
                        nc.scalar.activation(tmp[:, 2 + t % 2, :], tmp[:, t % 2, :], ACT.Silu).then_inc(gate_silu, 1)
                    else:
                        act.wait_ge(inner_done, n + 1)
                        nc.scalar.activation(mix_h[:, FC * (cs % 2) + t, :], tmp[:, 4 + t % 2, :], ACT.Copy)\
                            .then_inc(innerh_done, 1)
                    ahead(gu_slab(c) + i, gu_slab(cs) + i, units_ffn(c, i, False))

            def ahead(s, slot, units):
                if isinstance(s, int) and (s + WH < S_FFN + GU or s + WH >= N_SLABS):
                    if s + WH >= N_SLABS or s + WH < S_FFN + WH:
                        return
                high(s + WH, slot + WH, units)

            def down(c, cs):
                for i in range(DN):
                    ahead(dn_slab(c) + i, dn_slab(cs) + i, units_ffn(c, i, True))

            def y_copies(q):
                act.wait_ge(yt_done, q + 1)
                for j in (0, 2):
                    rows = P if j < 2 else TS
                    nc.scalar.activation(xtok[0:rows, j, 512 * q:512 * q + 512], mx[0:rows, j, :], ACT.Copy)\
                        .then_inc(yt_copied_a, 1)

            ffn_walk(act, gate_up, down)
            for q in range(4):
                y_copies(q)

        @block.vector
        def _(dve):
            seq = [0]

            def link(ins):
                seq[0] += 1
                ins.then_inc(dve_seq, 1)
                dve.wait_ge(dve_seq, seq[0])

            def low(s, slot, units):
                dve.wait_ge(high_done, s + 1)
                if units is not None:
                    dve.wait_ge(unit_done, units)
                nc.vector.tensor_tensor(wl[:, slot % WL, :], raw[:, slot % RAW, :], wh[:, slot % WH, :].bitcast(F32),
                                        ALU.subtract).then_inc(low_done, 1)

            def mean_square(rows, ps, width, n):
                nc.vector.tensor_scalar(rows, ps, 1.0 / width, EPS, ALU.mult, ALU.add).then_inc(ms_done, 1)
                dve.wait_ge(rt_done, n)

            def norm1():
                dve.wait_ge(ssq_done, KD)
                mean_square(tmp[:, 6, :], acc[0][:, 0:T], D, 1)
                link(nc.vector.reciprocal(tmp[:, 6, :], tmp[:, 6, :]))
                dve.wait_ge(consts_in, 16 * 9)

                def xn_low(k):
                    dve.wait_ge(acth_done, k + 1)
                    nc.vector.tensor_tensor(act_l[:, k, :], tmp[:, 2 + k % 4, :], act_h[:, k, :].bitcast(F32),
                                            ALU.subtract).then_inc(actl_done, 1)

                for k in range(KD):
                    if k >= 4:
                        dve.wait_ge(actl_done, k - 3)
                    nc.vector.scalar_tensor_tensor(out=tmp[:, 2 + k % 4, :], in0=xT[:, k, :],
                                                   scalar=gains[:, 0, k:k + 1], in1=tmp[:, 6, :],
                                                   op0=ALU.mult, op1=ALU.mult).then_inc(xn_done, 1)
                    if k >= 2:
                        xn_low(k - 2)
                    if k == 5:
                        low(0, 0, None)
                xn_low(KD - 2)
                xn_low(KD - 1)

            def lower_bound():
                x, d, e, r = (lbs[:, n, :] for n in range(4))
                link(nc.vector.tensor_copy(r, x))
                nc.vector.tensor_tensor(d, x, r, ALU.subtract).then_inc(lb_sub, 1)
                dve.wait_ge(lb_exp, 1)
                link(nc.vector.reciprocal(r, e))
                link(nc.vector.tensor_tensor(e, e, r, ALU.mult))
                link(nc.vector.tensor_tensor(e, e, e, ALU.subtract))
                link(nc.vector.tensor_scalar(x, e, LB_FLOOR, None, ALU.max))
                link(nc.vector.tensor_scalar(d, e, -1.0, 1.0, ALU.mult, ALU.add))

            def bias_by_distance():
                dve.wait_ge(lut_done, 1)
                nc.vector.tensor_copy(by_dist, mx[0:BH, 3, 0:384]).then_inc(lut_copied, 1)

            def bias_of_rows():
                dve.wait_ge(lut_done, 2)
                nc.vector.tensor_copy(s_bias, mx[:, 2, 0:132])
                nc.vector.tensor_copy(head_g[:, 3:4], mx[:, 2, 132:133]).then_inc(lut_copied, 1)
                link(nc.vector.tensor_scalar(head_g[:, 0:1], head_g[:, 0:1], SCALE, None, ALU.mult))
                nc.vector.tensor_copy(masks[:, :], masks_f).then_inc(masks_done, 1)

            def evacuate(s):
                ps = acc[s % 4][:, 0:T]
                if S_F <= s < S_Q:
                    h = s - S_F
                    dve.wait_ge(f_sig, h + 1)
                    nc.vector.tensor_scalar(f_a[:, h, :], f_a[:, h, :], lbs[:, 1, h:h + 1], lbs[:, 0, h:h + 1],
                                            ALU.mult, ALU.add)
                    nc.vector.tensor_scalar(k_a[:, h, :], k_a[:, h, :], lbs[:, 1, h:h + 1], None, ALU.mult)\
                        .then_inc(k_made, 1)
                elif S_Q <= s < S_I:
                    h = s - S_Q
                    dve.wait_ge(q_sig, h + 1)
                    nc.vector.tensor_tensor(q_a[:, h, :], ps, sig[:, h % 2, :], ALU.mult).then_inc(q_made, 1)
                elif S_G <= s < S_O:
                    h = s - S_G
                    dve.wait_ge(g_sig, h + 1)
                    nc.vector.tensor_tensor(reg_g[:, h, :], ps, sig[:, h % 2, :], ALU.mult).then_inc(g_made, 1)

            def qk_rows():
                dve.wait_ge(qk_ssq, 10)
                mean_square(norm_rows, mx[0:32, 0, 0:T], HD, 2)
                nc.vector.reciprocal(norm_rows, norm_rows).then_inc(rows_done, 1)

            def qk_norm():
                for i in range(10):
                    dst = reg_g[:, i, :] if i < 8 else kvT[:, i - 8, :]
                    g = head_g[:, 0:1] if i < 8 else head_g[:, 1:2]
                    dve.wait_ge(qk_bc, i + 1)
                    nc.vector.scalar_tensor_tensor(out=dst, in0=dst, scalar=g, in1=mx[:, 1 + i % 3, 0:T],
                                                   op0=ALU.mult, op1=ALU.mult).then_inc(qk_normed, 1)

            def softmax_front(n):
                k, j = divmod(n, 2)
                cols = slice(0, 2 * WIN) if j else slice(WIN, 2 * WIN)
                width = 2 * WIN if j else WIN
                sc = scores[:, n % 2, :, cols]
                mneg, es = st[:, n % 2, 1, :], st[:, n % 2, 2, :]
                dve.wait_ge(sc_done, n + 1)
                dve.wait_ge(bias_in[k % 2], 64 * (k // 2 + 1))
                if n >= 2:
                    dve.wait_ge(pt_done, n - 1)
                ps = mx[:, 0:2, :].rearrange("p a (b s) -> p (a b) s", b=2)[:, :, 0:width]
                nc.vector.tensor_tensor(sc, ps, bias_buf[k % 2][:, :, cols], ALU.add).then_inc(sc_biased, 1)
                dve.wait_ge(sc_biased, n + 1)
                link(nc.vector.tensor_reduce(st[:, n % 2, 0, :], sc, AX.X, ALU.max))
                sk = sinks[:, G * k:G * k + G].rearrange("p (gg par) -> p par gg", par=2)
                mx4 = st[:, n % 2, 0, :].rearrange("p (par gg) -> p par gg", par=2)
                link(nc.vector.tensor_tensor(mx4, mx4, sk, ALU.max))
                nc.vector.tensor_tensor(es.rearrange("p (par gg) -> p par gg", par=2), sk, mx4, ALU.subtract)
                nc.vector.tensor_scalar(mneg, st[:, n % 2, 0, :], -1.0, None, ALU.mult).then_inc(sc_max, 1)

            def softmax_back(n):
                dve.wait_ge(sc_exp, n + 1)
                link(nc.vector.tensor_tensor(st[:, n % 2, 3, :], st[:, n % 2, 3, :], st[:, n % 2, 2, :], ALU.add))
                nc.vector.reciprocal(st[:, n % 2, 4, :], st[:, n % 2, 3, :]).then_inc(sc_inv, 1)

            def out_low(n):
                k, j = divmod(n, 2)
                dve.wait_ge(mixh_done, n + 1)
                nc.vector.tensor_tensor(mix_l[:, 2 * k:2 * k + 2, P * j:P * j + P],
                                        mx[:, 2, 0:256].rearrange("p (m t) -> p m t", m=2),
                                        mix_h[:, 2 * k:2 * k + 2, P * j:P * j + P].bitcast(F32),
                                        ALU.subtract).then_inc(mixl_done, 1)

            def s_bias_place():
                dve.wait_ge(qr_zero, 2)
                for b in range(NB):
                    nc.vector.tensor_copy(s_bias_new[:, b, LB * b:LB * b + LB], s_bias[:, WIN:WIN + LB])\
                        .then_inc(sb_new, 1)

            def keys_copy(i):
                dve.wait_ge(kc_t, i + 1)
                if i == 0:
                    dve.wait_ge(sc_biased, 2 * KVH)
                else:
                    dve.wait_ge(ss_done, 2 * i)
                nc.vector.tensor_copy(kT_cache[:, :, :, 0:WIN],
                                      mx[:, 3, :].rearrange("p (n c s) -> p n c s", n=2, c=2)).then_inc(kc_copied, 1)

            def s_bias_add(n):
                b0, nb = 3 * n, min(3, NB - 3 * n)
                dve.wait_ge(ss_done, b0 + nb)
                if n == 0:
                    dve.wait_ge(sb_new, NB)
                    dve.wait_ge(pt_done, 2 * KVH)
                ps = mx[:, n, 0:3 * NK].rearrange("p (b s) -> p b s", b=3)[:, 0:nb, :]
                nc.vector.tensor_tensor(s_scores[:, b0:b0 + nb, 0:WIN], ps[:, :, 0:WIN],
                                        s_bias[:, 0:WIN].unsqueeze(1).broadcast_to([P, nb, WIN]), ALU.add)
                nc.vector.tensor_tensor(s_scores[:, b0:b0 + nb, WIN:NK], ps[:, :, WIN:NK],
                                        s_bias_new[:, b0:b0 + nb, :], ALU.add).then_inc(ss_biased, 1)

            def s_softmax_front():
                dve.wait_ge(ss_biased, 3)
                link(nc.vector.tensor_reduce(s_st[:, 0, :], s_scores, AX.X, ALU.max))
                link(nc.vector.tensor_scalar(s_st[:, 0, :], s_st[:, 0, :], head_g[:, 3:4], None, ALU.max))
                nc.vector.tensor_scalar(s_st[:, 1, :], s_st[:, 0, :], -1.0, None, ALU.mult)
                nc.vector.tensor_scalar(s_st[:, 2, :], s_st[:, 0, :], -1.0, head_g[:, 3:4], ALU.mult, ALU.add)\
                    .then_inc(ss_max, 1)

            def s_softmax_back():
                dve.wait_ge(ss_exp, 1)
                link(nc.vector.tensor_tensor(s_st[:, 3, :], s_st[:, 3, :], s_st[:, 2, :], ALU.add))
                link(nc.vector.reciprocal(s_st[:, 4, :], s_st[:, 3, :]))
                nc.vector.tensor_tensor(s_scores, s_scores, s_st[:, 4, :].unsqueeze(2).broadcast_to([P, NB, NK]),
                                        ALU.mult).then_inc(ss_probs, 1)

            def s_out_low():
                dve.wait_ge(so_copied, 2)
                nc.vector.tensor_tensor(mix_l[:, :, TP:T], s_out, mix_h[:, :, TP:T].bitcast(F32), ALU.subtract)\
                    .then_inc(mixl_done, 1)

            def level_merge(lv):
                mask = masks[:, P * lv:P * lv + P]
                for b in range(4):
                    dve.wait_ge(lv_done, lv_unit(lv, b) + 1)
                    if lv == 0 and b == 0:
                        dve.wait_ge(at_zero, 3)
                    if lv:
                        dve.wait_ge(lv_kept, lv_unit(lv - 1, b) + 1)
                    nc.vector.copy_predicated(
                        a_t[:, 2 * b:2 * b + 2, 0:3:2, :], mask.unsqueeze(1).unsqueeze(1).broadcast_to([P, 2, 2, P]),
                        mx[:, b, :].rearrange("p (h j t) -> p h j t", h=2, j=2)).then_inc(lv_kept, 1)
                if lv < 3:
                    dve.wait_ge(lv_done, lv_unit(lv, 4) + 1)
                    if lv:
                        dve.wait_ge(lv_kept, lv_unit(lv - 1, 4) + 1)
                    nc.vector.copy_predicated(
                        a_s, mask[0:TS, 0:TS].unsqueeze(1).broadcast_to([TS, AH, TS]),
                        mx[0:TS, 0, 0:256].rearrange("p (h t) -> p h t", h=AH)).then_inc(lv_kept, 1)

            def level_up(lv):
                n = LEVELS[lv]
                if lv == 0:
                    nc.vector.tensor_tensor(reg_qkf[:, 0:8 * T], reg_qkf[:, 0:8 * T], reg_qkf[:, 16 * T:24 * T],
                                            ALU.mult).then_inc(lv_next, 1)
                    return
                width = T if n < LB else TP
                def blocks(a):
                    return a[:, :, 0:width].rearrange("p h (b two n) -> p h b two n", two=2, n=n)
                nblk = width // (2 * n)
                fl, fr = blocks(f_a)[:, :, :, 0, 0:1], blocks(f_a)[:, :, :, 1, 0:1]
                q_r, k_l = blocks(q_a)[:, :, :, 1, :], blocks(k_a)[:, :, :, 0, :]
                if n == 1:
                    fb, fa = fl, fr
                else:
                    fb, fa = fl.broadcast_to([P, AH, nblk, n]), fr.broadcast_to([P, AH, nblk, n])
                nc.vector.tensor_tensor(q_r, q_r, fb, ALU.mult)
                link(nc.vector.tensor_tensor(k_l, k_l, fa, ALU.mult))
                nc.vector.tensor_tensor(fl, fl, fr, ALU.mult).then_inc(lv_next, 1)

            def next_level(lv):
                dve.wait_ge(lv_done, lv_units_through(lv))
                if lv:
                    dve.wait_ge(lv_next, lv)
                level_up(lv)

            def cross_copy():
                for b in range(2):
                    dve.wait_ge(lv_done, lv_units_through(7) + b + 1)
                    nc.vector.tensor_copy(a_t[:, 4 * b:4 * b + 4, 1, :],
                                          mx[:, b, :].rearrange("p (h t) -> p h t", h=4)).then_inc(lv_kept, 1)
                dve.wait_ge(lv_next, 8)
                nc.vector.tensor_tensor(k_a[:, :, 0:P], k_a[:, :, 0:P], f_a[:, :, P:P + 1].broadcast_to([P, AH, P]),
                                        ALU.mult).then_inc(lv_next, 1)

            def new_states(h):
                dve.wait_ge(s0_in[h % 2], 16 * (h // 2 + 1))
                for half in range(2):
                    dve.wait_ge(sm_st, 2 * h + half + 1)
                    for b in range(4 * half, 4 * half + 4):
                        s = s0[:, h % 2, b, :]
                        ins = nc.vector.scalar_tensor_tensor(
                            out=s, in0=s, scalar=f_a[:, h, TP + LB * b:TP + LB * b + 1],
                            in1=mx[:, 2 + half, P * (b % 4):P * (b % 4) + P], op0=ALU.mult, op1=ALU.add)
                    ins.then_inc(s0_new, 1)

            def h_norm_rows():
                dve.wait_ge(h_ssq, AH)
                dve.wait_ge(ps_done, AH // 2)
                mean_square(h_rows, mx[0:32, 0, 0:T], P, 3)
                nc.vector.reciprocal(h_rows, h_rows).then_inc(h_rowsd, 1)

            def h_out(heads):
                def gate(h):
                    dve.wait_ge(h_normed, h + 1)
                    nc.vector.tensor_tensor(q_a[:, h, :], q_a[:, h, :], reg_g[:, h, :], ALU.mult).then_inc(h_gated, 1)

                def lows(h):
                    dve.wait_ge(hh_done, h + 1)
                    nc.vector.tensor_tensor(act_l[:, h, :], q_a[:, h, :], act_h[:, h, :].bitcast(F32),
                                            ALU.subtract).then_inc(hl_done, 1)

                for h in heads:
                    dve.wait_ge(h_bc, h + 1)
                    nc.vector.scalar_tensor_tensor(out=q_a[:, h, :], in0=q_a[:, h, :], scalar=head_g[:, 2:3],
                                                   in1=mx[:, 1 + h % 3, 0:T], op0=ALU.mult, op1=ALU.mult)\
                        .then_inc(h_normed, 1)
                    gate(h)
                for h in heads:
                    lows(h)

            def add_unit(u):
                m = u % 16
                if u == 0:
                    dve.wait_ge(reloaded, 16)
                if u >= 16:
                    dve.wait_ge(x_added, m + 1)
                dve.wait_ge(unit_done, U_O + u + 1)
                nc.vector.tensor_tensor(xT[:, m, :], acc[(U_O + u) % 4][:, 0:T], xT[:, m, :], ALU.add)\
                    .then_inc(x_added, 1)

            def gained(m):
                dve.wait_ge(x_added, 17 + m)
                if m == 0:
                    dve.wait_ge(ps_out, 16 * AH // 2)
                if m >= 4:
                    dve.wait_ge(xgl_done, m - 3)
                nc.vector.tensor_scalar(tmp[:, 2 + m % 4, :], xT[:, m, :], gains[:, 1, m:m + 1], None, ALU.mult)\
                    .then_inc(xg_done, 1)

            def gained_low(m):
                dve.wait_ge(xgh_done, m + 1)
                nc.vector.tensor_tensor(act_l[:, m, :], tmp[:, 2 + m % 4, :], act_h[:, m, :].bitcast(F32),
                                        ALU.subtract).then_inc(xgl_done, 1)

            norm1()
            lower_bound()
            low(1, 1, None)
            for s in range(S_FFN):
                if 0 <= s - S_AT < 8:
                    softmax_front(s - S_AT)
                if 0 <= s - S_AT - 2 < 8:
                    out_low(s - S_AT - 2)
                if 0 <= s - S_AT < 8:
                    softmax_back(s - S_AT)
                if s == S_QKN - 1:
                    qk_rows()
                if s == S_QKN:
                    qk_norm()
                if s == S_LUT:
                    bias_by_distance()
                if s == S_LUT + 1:
                    bias_of_rows()
                if s == S_SA - 1:
                    s_bias_place()
                if S_SA <= s <= S_SA + 1:
                    keys_copy(2 * (s - S_SA))
                    keys_copy(2 * (s - S_SA) + 1)
                if s == S_SA + 1:
                    s_bias_add(0)
                if s == S_SA + 2:
                    s_bias_add(1)
                    s_bias_add(2)
                    s_softmax_front()
                    s_softmax_back()
                if s == S_SA + 4:
                    s_out_low()
                if 0 <= s - S_SM - 1 < AH:
                    new_states(s - S_SM - 1)
                if 0 <= s - S_LV < 8:
                    level_merge(s - S_LV)
                    next_level(s - S_LV)
                if s == S_LV + 8:
                    cross_copy()
                if s == S_HN + 1:
                    h_norm_rows()
                if s in (S_HN + 2, S_HN + 3):
                    h_out(range(4 * (s - S_HN - 2), 4 * (s - S_HN - 1)))
                if s < S_O:
                    evacuate(s)
                if S_O <= s:
                    for u in (2 * (s - S_O), 2 * (s - S_O) + 1):
                        add_unit(u)
                low(s + WL, s + WL, units_through(s))
            for m in range(KD):
                gained(m)
                if m >= 2:
                    gained_low(m - 2)
            gained_low(KD - 2)
            gained_low(KD - 1)
            dve.wait_ge(ssq2_done, 1)
            mean_square(rstd2, mx[:, 0, 0:T], D, 4)
            nc.vector.reciprocal(rstd2, rstd2).then_inc(rstd2_done, 1)
            dve.wait_ge(rstd2_done, 1)

            def gate_up(c, cs):
                for i in range(GU):
                    t, up = divmod(i, 2)
                    n = c * FC + t
                    ps = acc[bank_gu(cs, i)][:, 0:T]
                    dve.wait_ge(unit_done, units_ffn(c, i, False))
                    if not up:
                        if not (isinstance(c, int) and c == 0 and t < 2):
                            dve.wait_ge(gate_silu, n - 1)
                        nc.vector.tensor_tensor(tmp[:, t % 2, :], ps, rstd2, ALU.mult).then_inc(gate_scaled, 1)
                        dve.wait_ge(gate_silu, n + 1)
                        nc.vector.tensor_tensor(tmp[:, 2 + t % 2, :], tmp[:, 2 + t % 2, :], rstd2, ALU.mult)\
                            .then_inc(gate_ready, 1)
                    else:
                        dve.wait_ge(gate_ready, n + 1)
                        if not (isinstance(c, int) and c == 0 and t < 2):
                            dve.wait_ge(innerl_done, n - 1)
                        nc.vector.tensor_tensor(tmp[:, 4 + t % 2, :], ps, tmp[:, 2 + t % 2, :], ALU.mult)\
                            .then_inc(inner_done, 1)
                        dve.wait_ge(innerh_done, n + 1)
                        slot = FC * (cs % 2) + t
                        nc.vector.tensor_tensor(mix_l[:, slot, :], tmp[:, 4 + t % 2, :],
                                                mix_h[:, slot, :].bitcast(F32), ALU.subtract)\
                            .then_inc(innerl_done, 1)
                    ahead(gu_slab(c) + i, gu_slab(cs) + i, units_ffn(c, i, False))

            def ahead(s, slot, units):
                if isinstance(s, int) and s + WL >= N_SLABS:
                    return
                low(s + WL, slot + WL, units)

            def y_copy(q):
                dve.wait_ge(yt_done, q + 1)
                nc.vector.tensor_copy(xtok[:, 1, 512 * q:512 * q + 512], mx[:, 1, :]).then_inc(yt_copied_v, 1)

            def down(c, cs):
                for i in range(DN):
                    if i and isinstance(c, int) and c == NCH - 1:
                        y_copy(i - 1)
                    for n in range(4):
                        m = 4 * i + n
                        if not (isinstance(c, int) and c == 0):
                            dve.wait_ge(down_added, 16 * c - 15 + m)
                        dve.wait_ge(unit_done, units_ffn(c, i, True) - 3 + n)
                        nc.vector.tensor_tensor(xT[:, m, :], acc[n][:, 0:T], xT[:, m, :], ALU.add)\
                            .then_inc(down_added, 1)
                    ahead(dn_slab(c) + i, dn_slab(cs) + i, units_ffn(c, i, True))

            ffn_walk(dve, gate_up, down)
            y_copy(3)

        @block.tensor
        def _(pe):
            mm = nc.tensor.matmul

            def x_transpose(k):
                if k >= 4:
                    pe.wait_ge(sq_done, k - 3)
                for j in range(NTT):
                    rows = P if j < 2 else TS
                    ins = nc.tensor.transpose(mx[:, k % 4, P * j:P * j + rows], xtok[0:rows, j, P * k:P * k + P],
                                              ident[0:rows, 0:rows])
                ins.then_inc(xt_done, 1)

            def x_ssq(k):
                pe.wait_ge(sq_done, k + 1)
                mm(acc[0][:, 0:T], ones[:, :], tmp[:, k % 2, :], start=(k == 0), stop=(k == KD - 1))\
                    .then_inc(ssq_done, 1)

            pe.wait_ge(x_in, 48)
            pe.wait_ge(small_in, 16)
            pe.wait_ge(ones_set, 1)
            for k in range(KD + 2):
                if k < KD:
                    x_transpose(k)
                if k >= 2:
                    x_ssq(k - 2)

            def bias_by_distance():
                pe.wait_ge(early_in, 64)
                pe.wait_ge(at_zero, 1)
                mm(mx[0:BH, 3, 0:384], table[:, :], early[0:33, 0:384], start=True, stop=True).then_inc(lut_done, 1)

            def bias_of_rows():
                pe.wait_ge(lut_copied, 1)
                for l in range(LB):
                    mm(mx[:, 2, 0:132], early[0:BH, 384 + P * l:384 + P * l + P], by_dist[:, 127 - l:127 - l + 132],
                       start=(l == 0), stop=(l == LB - 1))
                for l in range(LB):
                    ins = mm(mx[:, 2, 132:133], early[0:BH, 384 + P * l:384 + P * l + P], sink_col,
                             start=(l == 0), stop=(l == LB - 1))
                ins.then_inc(lut_done, 1)

            def passes(bank, slot, k, cols, a_hi, a_lo, ready, between):
                w_h = wh[:, slot % WH, :].rearrange("p (k c) -> p k c", k=k)
                w_l = wl[:, slot % WL, :].rearrange("p (k c) -> p k c", k=k)
                out = acc[bank][:, 0:T]
                for i in range(k):
                    ready(i)
                    mm(out, w_h[:, i, cols], a_hi[:, i, :], start=(i == 0), stop=False)
                    mm(out, w_h[:, i, cols], a_lo[:, i, :], start=False, stop=False)
                between()
                for i in range(k):
                    ins = mm(out, w_l[:, i, cols], a_hi[:, i, :], start=False, stop=(i == k - 1))
                ins.then_inc(unit_done, 1)

            def qk_squares(i):
                pe.wait_ge(qk_sq, i + 1)
                mm(mx[0:32, 0, 0:T], pair_win[:, 32 - 2 * i:64 - 2 * i], tmp[:, i % 2, :],
                   start=(i == 0), stop=(i == 9)).then_inc(qk_ssq, 1)

            def qk_broadcast():
                pe.wait_ge(rows_done, 1)
                pe.wait_ge(rows_spread, 1)
                for i in range(10):
                    if i >= 3:
                        pe.wait_ge(qk_normed, i - 2)
                    mm(mx[:, 1 + i % 3, 0:T], head_rows[:, P * i:P * i + P], norm_rows, start=True, stop=True)\
                        .then_inc(qk_bc, 1)

            def token_major():
                pe.wait_ge(qkv_done, 12)
                for c in range(2):
                    for j in range(2):
                        ins = nc.tensor.transpose(mx[:, 0, 256 * j + P * c:256 * j + P * c + P],
                                                  kvT[:, 2 + c, P * j:P * j + P], ident)
                ins.then_inc(vk_t, 1)
                pe.wait_ge(qk_normed, 10)
                for c in range(2):
                    nc.tensor.transpose(mx[0:TS, 1, P * c:P * c + P], kvT[:, 2 + c, TP:T], ident)
                    nc.tensor.transpose(mx[0:TS, 1, 256 + P * c:256 + P * c + P], kvT[:, c, TP:T], ident)
                    ins = nc.tensor.transpose(mx[:, 2, P * c:P * c + P], kvT[:, c, P:TP], ident)
                ins.then_inc(vk_t, 1)

            def prompt_scores(n):
                k, j = divmod(n, 2)
                width = 2 * WIN if j else WIN
                if n == 0:
                    pe.wait_ge(k_copied, 8)
                    pe.wait_ge(vk_tok, 3)
                else:
                    pe.wait_ge(sc_biased, n)
                for g in range(G):
                    par, gg = g % 2, g // 2
                    half = slice(HD * par, HD * par + HD)
                    ins = mm(mx[:, par, 256 * gg:256 * gg + width], reg_g[half, 2 * k + gg, P * j:P * j + P],
                             k_both[half, k, 0:width], start=True, stop=True)
                ins.then_inc(sc_done, 1)

            def probs_transpose(n):
                j = n % 2
                pe.wait_ge(sc_probs, n + 1)
                if n:
                    if n % 2:
                        pe.wait_ge(mixl_done, n)
                    pe.wait_ge(pt_copied, n)
                else:
                    pe.wait_ge(vk_tok, 3)
                for blk in range(1 - j, 2):
                    for h in range(G):
                        ins = nc.tensor.transpose(mx[:, 2 + blk, P * h:P * h + P],
                                                  scores[:, n % 2, h, P * blk:P * blk + P], ident)
                ins.then_inc(pt_done, 1)

            def prompt_out(n):
                k, j = divmod(n, 2)
                pe.wait_ge(pt_copied, n + 1)
                if n:
                    pe.wait_ge(mixl_done, n)
                for g in range(G):
                    par, gg = g % 2, g // 2
                    for blk in range(1 - j, 2):
                        ins = mm(mx[HD * par:HD * par + HD, 2, P * gg:P * gg + P],
                                 v_tok[:, j - 1 + blk, HD * k:HD * k + HD],
                                 probs_t[:, blk, 2 * par + gg, :], start=(blk == 1 - j), stop=(blk == 1))
                ins.then_inc(pv_done, 1)

            def sampled_scores(i):
                if i == 0:
                    pe.wait_ge(pt_copied, 2 * KVH)
                    pe.wait_ge(mixl_done, 2 * KVH)
                    pe.wait_ge(qr_done, 16)
                    pe.wait_ge(kn_copied, 2)
                else:
                    pe.wait_ge(kc_copied, i)
                    for b in (2 * i - 2, 2 * i - 1):
                        for k in range(KVH):
                            ins = mm(mx[32 * k:32 * k + 32, b // 3, NK * (b % 3):NK * (b % 3) + NK],
                                     q_rows[:, k, b, :], kT_cache[:, b % 2, k // 2, :], start=True, stop=True)
                        ins.then_inc(ss_done, 1)
                if i < NB // 2:
                    pe.wait_ge(kc_in[i % 2], 32 * (i // 2 + 1))
                    for n in range(2):
                        for c in range(2):
                            ins = nc.tensor.transpose(mx[:, 3, 256 * n + P * c:256 * n + P * c + P],
                                                      k_cache[i % 2][:, n, P * c:P * c + P], ident)
                    ins.then_inc(kc_t, 1)

            def sampled_probs():
                pe.wait_ge(ss_probs, 1)
                for n in range(2):
                    for b in range(4 * n, 4 * n + 4):
                        nc.tensor.transpose(mx[:, 2 * n, P * (b % 4):P * (b % 4) + P], s_scores[:, b, 0:WIN], ident)
                        ins = nc.tensor.transpose(mx[0:TS, 2 * n + 1, P * (b % 4):P * (b % 4) + P],
                                                  s_scores[:, b, WIN:NK], ident)
                    ins.then_inc(sp_t, 1)

            def sampled_out():
                pe.wait_ge(sp_copied, 2)
                pe.wait_ge(vc_in, 16)
                out = mx[0:HD, 0, :].rearrange("p (k b m) -> p k b m", k=KVH, b=NB)
                for k in range(KVH):
                    mm(out[:, k], v_tok[0:TS, 2, HD * k:HD * k + HD], s_new_t[:, :, 32 * k:32 * k + 16],
                       start=True, stop=True)
                    for b in range(NB):
                        ins = mm(out[:, k, b], v_cache[:, b, HD * k:HD * k + HD], s_probs_t[:, b, 32 * k:32 * k + 16],
                                 start=False, stop=True, skip_group_check=True)
                ins.then_inc(so_done, 1)

            def level(lv):
                pe.wait_ge(lv_next, lv) if lv else None
                if lv == 0:
                    pe.wait_ge(q_made, AH)
                    pe.wait_ge(k_made, AH)
                    pe.wait_ge(so_copied, 2)
                mixer_banks_free(S_LV + lv)
                for b in range(4):
                    if b == 2 and S_LV + lv > S_SM:
                        pe.wait_ge(s0_new, 2 * (S_LV + lv - S_SM))
                    if lv:
                        pe.wait_ge(lv_kept, lv_unit(lv - 1, 4 if b == 0 and lv <= 3 else b) + 1)
                    for i in range(4):
                        h, j = 2 * b + i // 2, i % 2
                        ins = mm(mx[:, b, P * i:P * i + P], k_a[:, h, P * j:P * j + P], q_a[:, h, P * j:P * j + P],
                                 start=True, stop=True)
                    ins.then_inc(lv_done, 1)
                if lv < 3:
                    pe.wait_ge(lv_kept, lv_unit(lv, 0) + 1)
                    for h in range(AH):
                        ins = mm(mx[0:TS, 0, TS * h:TS * h + TS], k_a[:, h, TP:T], q_a[:, h, TP:T],
                                 start=True, stop=True)
                    ins.then_inc(lv_done, 1)

            def mixer_banks_free(s):
                if s > S_VT:
                    pe.wait_ge(v_tokd, min(s - S_VT, AH))
                if s > S_SM:
                    n = min(s - S_SM, AH)
                    pe.wait_ge(kt_copied, n)
                    pe.wait_ge(sm_oc, n)

            def cross():
                pe.wait_ge(lv_next, 8)
                mixer_banks_free(S_LV + 8)
                for b in range(2):
                    pe.wait_ge(lv_kept, lv_unit(7, b) + 1)
                    for i in range(4):
                        h = 4 * b + i
                        ins = mm(mx[:, b, P * i:P * i + P], k_a[:, h, 0:P], q_a[:, h, P:TP], start=True, stop=True)
                    ins.then_inc(lv_done, 1)

            def levels_kept(s):
                if s >= S_LV:
                    n = min(s - S_LV, 8)
                    pe.wait_ge(lv_kept, lv_units_through(n) if n < 8 else lv_units_through(7) + 2)

            def v_transpose(h):
                levels_kept(S_VT + h)
                pe.wait_ge(i_copied, h + 1)
                for j in range(NTT):
                    rows = P if j < 2 else TS
                    ins = nc.tensor.transpose(mx[0:rows, 0, P * j:P * j + P], iT[:, h % 2, P * j:P * j + rows], ident)
                ins.then_inc(v_t, 1)

            def sampled_head(h):
                levels_kept(S_SM + h)
                if h:
                    pe.wait_ge(sm_oc, h)
                    pe.wait_ge(kt_copied, h)
                nc.tensor.transpose(mx[0:TS, 1, 128:256], k_a[:, h, TP:T], ident)
                pe.wait_ge(v_tokd, h + 1)
                pe.wait_ge(s0_in[h % 2], 16 * (h // 2 + 1))
                mm(mx[:, 1, 0:TS], v_a[0:TS, 2, P * h:P * h + P], a_s[:, h, :], start=True, stop=True)
                for b in range(NB):
                    ins = mm(mx[:, 1, LB * b:LB * b + LB], s0[:, h % 2, b, :], q_a[:, h, TP + LB * b:TP + LB * b + LB],
                             start=False, stop=True, skip_group_check=True)
                ins.then_inc(sm_o, 1)

            def sampled_states(h):
                levels_kept(S_SM + h)
                pe.wait_ge(kt_copied, h + 1)
                pe.wait_ge(v_owned, h + 1)
                if h:
                    pe.wait_ge(s0_new, 2 * h)
                for half in range(2):
                    mm(mx[:, 2 + half, :], kt_s[:, h % 2, :],
                       v_own[:, h % 2, 4 * half:4 * half + 4, :].rearrange("p b v -> p (b v)"),
                       start=True, stop=True).then_inc(sm_st, 1)

            def prompt_head(h):
                if h < 2:
                    pe.wait_ge(lv_kept, lv_units_through(7) + 2)
                    pe.wait_ge(sm_oc, AH)
                    pe.wait_ge(v_tokd, AH)
                else:
                    pe.wait_ge(po_copied, h - 1)
                mm(mx[:, h % 2, 0:TP], v_a[:, 0, P * h:P * h + P],
                   a_t[:, h, 0:2, :].rearrange("p n t -> p (n t)"), start=True, stop=True)
                mm(mx[:, h % 2, P:TP], v_a[:, 1, P * h:P * h + P], a_t[:, h, 2, :], start=False, stop=True,
                   skip_group_check=True).then_inc(po_done, 1)

            def prompt_states(i):
                if i == 0:
                    pe.wait_ge(lv_next, 9)
                    pe.wait_ge(s0_new, 2 * AH)
                else:
                    pe.wait_ge(ps_copied, i)
                for h in (2 * i, 2 * i + 1):
                    for j in range(2):
                        ins = nc.tensor.transpose(mx[:, 2, 256 * (h % 2) + P * j:256 * (h % 2) + P * j + P],
                                                  k_a[:, h, P * j:P * j + P], ident)
                ins.then_inc(ktp_done, 1)
                pe.wait_ge(ktp_copied, i + 1)
                for h in (2 * i, 2 * i + 1):
                    for j in range(2):
                        ins = mm(mx[:, 3, P * (h % 2):P * (h % 2) + P], kt_p[:, h % 2, j, :],
                                 v_a[:, j, P * h:P * h + P], start=(j == 0), stop=(j == 1))
                ins.then_inc(ps_done, 1)

            def h_squares(heads):
                pe.wait_ge(po_copied, AH)
                for h in heads:
                    pe.wait_ge(h_sq, h + 1)
                    mm(mx[0:32, 0, 0:T], whole_win[:, 32 - 2 * h:64 - 2 * h], sig[:, h % 2, :],
                       start=(h == 0), stop=(h == AH - 1)).then_inc(h_ssq, 1)

            def h_broadcast(heads):
                pe.wait_ge(h_rowsd, 1)
                pe.wait_ge(ps_copied, AH // 2)
                for h in heads:
                    if h >= 3:
                        pe.wait_ge(h_normed, h - 2)
                    mm(mx[:, 1 + h % 3, 0:T], ident[0:32, 2 * h:2 * h + 1].broadcast_to([32, P]), h_rows, start=True, stop=True).then_inc(h_bc, 1)

            def x2_ssq():
                pe.wait_ge(sq2_done, 2 * KD - 1)
                mm(mx[:, 0, 0:T], ones[:, :], tmp[:, 0, :], start=True, stop=True).then_inc(ssq2_done, 1)

            def at_start(s):
                if s == S_LUT:
                    bias_by_distance()
                if s == S_LUT + 1:
                    bias_of_rows()
                if s == S_QKN:
                    qk_broadcast()
                if 0 <= s - S_AT < 8:
                    prompt_scores(s - S_AT)
                if 0 <= s - S_AT - 2 < 8:
                    prompt_out(s - S_AT - 2)
                if S_SA <= s <= S_SA + 2:
                    sampled_scores(2 * (s - S_SA))
                if 0 <= s - S_SM - 1 < AH:
                    sampled_states(s - S_SM - 1)
                if 0 <= s - S_LV < 8:
                    level(s - S_LV)
                if s == S_LV + 8:
                    cross()
                if 0 <= s - S_PO < 4:
                    prompt_head(2 * (s - S_PO))
                    prompt_head(2 * (s - S_PO) + 1)
                if s in (S_HN, S_HN + 1):
                    h_squares(range(4 * (s - S_HN), 4 * (s - S_HN) + 2))
                if s in (S_HN + 2, S_HN + 3):
                    h_broadcast(range(4 * (s - S_HN - 2), 4 * (s - S_HN - 2) + 2))

            def in_the_middle(s):
                if 2 <= s < 12:
                    qk_squares(s - 2)
                if s == S_QKN:
                    token_major()
                if 0 <= s - S_AT - 1 < 8:
                    probs_transpose(s - S_AT - 1)
                if S_SA <= s <= S_SA + 1:
                    sampled_scores(2 * (s - S_SA) + 1)
                if s == S_SA + 3:
                    sampled_probs()
                if s == S_SA + 4:
                    sampled_out()
                if 0 <= s - S_VT < AH:
                    v_transpose(s - S_VT)
                if 0 <= s - S_SM < AH:
                    sampled_head(s - S_SM)
                if 0 <= s - S_PS < 4:
                    prompt_states(s - S_PS)
                if s in (S_HN, S_HN + 1):
                    h_squares(range(4 * (s - S_HN) + 2, 4 * (s - S_HN) + 4))
                if s in (S_HN + 2, S_HN + 3):
                    h_broadcast(range(4 * (s - S_HN - 2) + 2, 4 * (s - S_HN - 2) + 4))

            def unit_free(u):
                p = u - 4
                if p < 0:
                    pe.wait_ge(ms_done, 1) if u == 0 else None
                elif p < S_F:
                    pe.wait_ge(qkv_done, p + 1)
                elif p < S_Q:
                    pe.wait_ge(f_sig, p - S_F + 1)
                elif p < S_I:
                    pe.wait_ge(q_made, p - S_Q + 1)
                elif p < S_G:
                    pe.wait_ge(i_copied, p - S_I + 1)
                elif p < S_O:
                    pe.wait_ge(g_made, p - S_G + 1)
                elif p < U_FFN:
                    pe.wait_ge(x_added, p - U_O + 1)

            for s in range(S_FFN):
                at_start(s)
                pe.wait_ge(high_done, s + 1)

                def low_parts(first):
                    if first:
                        pe.wait_ge(low_done, s + 1)

                if s < S_O:
                    unit_free(s)

                    def ready(i):
                        if s == 0:
                            pe.wait_ge(actl_done, i + 1)

                    def between():
                        in_the_middle(s)
                        low_parts(True)

                    passes(s % 4, s, KD, slice(0, P), act_h, act_l, ready, between)
                else:
                    hgrn = s >= S_O2
                    if s == S_O:
                        pe.wait_ge(mixl_done, 2 * KVH + 1)
                    if s == S_O2:
                        pe.wait_ge(hl_done, AH)
                    for n in range(2):
                        u = U_O + 2 * (s - S_O) + n
                        unit_free(u)
                        a_hi, a_lo = (act_h, act_l) if hgrn else (mix_h, mix_l)
                        passes(u % 4, s, 8, slice(P * n, P * n + P), a_hi, a_lo, lambda i: None,
                               lambda: low_parts(n == 0))
                        if n == 0:
                            in_the_middle(s)

            def gate_up(c, cs):
                for i in range(GU):
                    t, up = divmod(i, 2)
                    bank = bank_gu(cs, i)
                    if i >= 4:
                        n = c * FC + (i - 4) // 2
                        pe.wait_ge(inner_done if up else gate_scaled, n + 1)
                    elif isinstance(c, int) and c == 0:
                        pe.wait_ge(x_added, 29 + i)
                    elif isinstance(c, int) and c == 1:
                        pe.wait_ge(inner_done if up else gate_scaled, 2 + i // 2 + 1)
                    else:
                        pe.wait_ge(down_added, 16 * (c - 2) + 12 + i + 1)
                    s = gu_slab(c) + i
                    pe.wait_ge(high_done, s + 1)

                    def ready(k):
                        if isinstance(c, int) and c == 0 and i == 0:
                            pe.wait_ge(xgl_done, k + 1)

                    def between():
                        if isinstance(c, int) and c == 0 and i == 0:
                            x2_ssq()
                        pe.wait_ge(low_done, s + 1)

                    passes(bank, gu_slab(cs) + i, KD, slice(0, P), act_h, act_l, ready, between)

            def y_group(q):
                pe.wait_ge(down_added, 16 * (NCH - 1) + 4 * q + 4)
                if q:
                    pe.wait_ge(yt_copied_a, 2 * q)
                    pe.wait_ge(yt_copied_v, q)
                for j in range(NTT):
                    rows = P if j < 2 else TS
                    for i in range(4):
                        ins = nc.tensor.transpose(mx[0:rows, j, P * i:P * i + P], xT[:, 4 * q + i, P * j:P * j + rows],
                                                  ident)
                ins.then_inc(yt_done, 1)

            def down(c, cs):
                half = FC * (cs % 2)
                pe.wait_ge(innerl_done, FC * c + FC)
                for i in range(DN):
                    s = dn_slab(c) + i
                    pe.wait_ge(high_done, s + 1)
                    for n in range(4):
                        m = 4 * i + n
                        if m >= 4:
                            pe.wait_ge(down_added, 16 * c + m - 3)
                        elif isinstance(c, int) and c == NCH - 1:
                            pe.wait_ge(down_added, 16 * (c - 1) + 12 + n + 1)
                        else:
                            pe.wait_ge(inner_done if n % 2 else gate_scaled, (c + 1) * FC + 2 + n // 2 + 1)
                        passes(n, dn_slab(cs) + i, FC, slice(P * n, P * n + P), mix_h[:, half:half + FC, :],
                               mix_l[:, half:half + FC, :], lambda k: None,
                               lambda: pe.wait_ge(low_done, s + 1) if n == 0 else None)
                        if n == 1 and i and isinstance(c, int) and c == NCH - 1:
                            y_group(i - 1)

            ffn_walk(pe, gate_up, down)
            y_group(3)


def bank_gu(c, i):
    return i % 4


def lv_unit(lv, b):
    return 4 * lv + min(lv, 3) + b


def lv_units_through(lv):
    return lv_unit(lv + 1, 0)


_INS = ['x_prompt', 'x_sample', 'cache_k', 'cache_v', 'state_hgrn', 'norm_mix', 'w_in', 'lower_bounds', 'hgrn_norm',
        'q_norm', 'k_norm', 'attn_sinks', 'rel_bias_table', 'w_out', 'norm_ffn', 'w_gate', 'w_up', 'w_down']
_OUTS = [(1, TP, D), (NB, LB, D), (1, 1, WIN, KVH, HD), (1, 1, WIN, KVH, HD), (1, 1, AH, P, P),
         (1, NB, WIN, KVH, HD), (1, NB, WIN, KVH, HD), (1, NB, AH, P, P)]


def kernel(**inputs):
    import numpy as _np
    import concourse.bacc as _bacc
    from concourse import mybir as _mybir
    from concourse.bass_utils import run_bass_kernel_spmd as _run

    nc = _bacc.Bacc("TRN2", target_bir_lowering=False, num_devices=1)
    arrays, args = {}, []
    for name in _INS:
        a = _np.ascontiguousarray(inputs[name])
        arrays[f"in_{name}_dram"] = a
        args.append(nc.dram_tensor(f"in_{name}_dram", a.shape, _mybir.dt.from_np(a.dtype), kind="ExternalInput").ap())
    for name, a in zip(("small", "masks", "early"), constants()):
        arrays[f"const_{name}_dram"] = a
        args.append(nc.dram_tensor(f"const_{name}_dram", a.shape, _mybir.dt.from_np(a.dtype), kind="ExternalInput").ap())
    for i, shape in enumerate(_OUTS):
        args.append(nc.dram_tensor(f"out_{i}_dram", shape, F32, kind="ExternalOutput").ap())
    layer_kernel(nc, *args)
    r = _run(nc, [arrays], core_ids=[0])
    return tuple(r.results[0][f"out_{i}_dram"] for i in range(len(_OUTS)))
```

```python
import math
from contextlib import ExitStack

import numpy as np

import concourse.bass as bass
from concourse import mybir

F32 = mybir.dt.float32
F32R = mybir.dt.float32r
U8 = mybir.dt.uint8
ALU = mybir.AluOpType
ACT = mybir.ActivationFunctionType
AX = mybir.AxisListType

P = 128
D = 2048
KD = D // P
TP = 256
NB, LB = 8, 4
TS = NB * LB
T = TP + TS
NTT = 3
AH = 8
BH, KVH, G, HD = 16, 4, 4, 64
WIN = 128
F = 5632
EPS = 1e-6
SCALE = 1.0 / math.sqrt(HD)
NEG = -1e30
LB_FLOOR = 1e-20
N_BUCKETS, MAX_DISTANCE = 32, 128

B_Q, B_K, B_V = 8, 2, 2
COL0 = 4096
IN_COLS = ([COL0 + P * i for i in range(12)] + [1024 + P * i for i in range(8)] + [P * i for i in range(8)]
           + [2048 + P * i for i in range(8)] + [3072 + P * i for i in range(8)])
S_F, S_Q, S_I, S_G, S_O, S_O2, S_FFN = 12, 20, 28, 36, 44, 52, 60
FC = 4
NCH = F // (FC * P)
GU, DN = 2 * FC, 4
N_SLABS = S_FFN + NCH * (GU + DN)
RAW, WH, WL = 3, 3, 2
SLAB = 2048
U_O = 44
U_FFN = U_O + 32

S_LUT = 4
S_LB = 8
S_QKN = 12
S_AT = 14
S_SA = 24
S_LV = 29
S_VT = 30
S_SM = 32
S_PO = 40
S_PS = 41
S_HN = 45
TOKEN_OUTS = 4 + 2 * NB
KEYS_FIRST = [8, 9, 0, 1, 2, 3, 4, 5, 6, 7]
LEVELS = [0, 1, 2, 4, 8, 16, 32, 64]


def t5_bucket(dist):
    n = np.maximum(dist, 0)
    max_exact = N_BUCKETS // 2
    nf = np.maximum(n, 1).astype(np.float32)
    large = max_exact + (np.log(nf / max_exact) / math.log(MAX_DISTANCE / max_exact)
                         * (N_BUCKETS - max_exact)).astype(np.int32)
    return np.where(n < max_exact, n, np.minimum(large, N_BUCKETS - 1)).astype(np.int32)


def constants():
    ident = np.eye(P, dtype=np.float32)
    pair_win = np.zeros((P, 64), np.float32)
    pair_win[np.arange(P), 32 + np.arange(P) // HD] = 1
    whole_win = np.zeros((P, 64), np.float32)
    whole_win[:, 32:34] = 1
    own = np.zeros((P, NB), np.float32)
    own[np.arange(TS), np.arange(TS) // LB] = 1
    small = np.concatenate([ident, pair_win, whole_win, own], axis=1)
    s, t = np.meshgrid(np.arange(P), np.arange(P), indexing="ij")
    masks = np.stack([(s == t) if lv == 0 else
                      ((s // (2 * lv) == t // (2 * lv)) & (s // lv % 2 == 0) & (t // lv % 2 == 1))
                      for lv in LEVELS], axis=1).astype(np.float32).reshape(P, -1)
    dist = 255 - np.arange(384)
    ok = (dist >= 0) & (dist < WIN)
    row = np.where(ok, t5_bucket(dist), N_BUCKETS)
    bucket_of = (np.arange(33)[:, None] == row[None]).astype(np.float32)
    rows_of = np.zeros((BH, LB, P), np.float32)
    for h in range(BH):
        for l in range(LB):
            rows_of[h, l, 32 * (h // G) + LB * (h % G) + l] = 1
    early = np.zeros((P, 384 + LB * P), np.float32)
    early[0:33, 0:384] = bucket_of
    early[0:BH, 384:] = rows_of.reshape(BH, -1)
    return small, masks, early


def layer_kernel(nc, x_prompt, x_sample, cache_k, cache_v, state_hgrn, norm_mix, w_in, lower_bounds, hgrn_norm,
                 q_norm, k_norm, attn_sinks, rel_bias_table, w_out, norm_ffn, w_gate, w_up, w_down,
                 c_small, c_masks, c_early,
                 y_prompt, y_sample, prompt_k, prompt_v, prompt_state, sample_k, sample_v, sample_state):
    w_in, w_out, w_gate, w_up, w_down = w_in[0], w_out[0], w_gate[0], w_up[0], w_down[0]
    win_v = w_in.rearrange("(k p) c -> p k c", p=P)
    wout_v = w_out.rearrange("(k p) c -> p k c", p=P)
    wg_v = w_gate.rearrange("(k p) c -> p k c", p=P)
    wu_v = w_up.rearrange("(k p) c -> p k c", p=P)
    x_spill = nc.dram_tensor("x_spill", (P, KD * T), F32).ap()
    bias_rows = nc.dram_tensor("bias_rows", (BH, P, 384), F32).ap()

    with ExitStack() as ctx:
        def sb(name, shape, dt=F32):
            return ctx.enter_context(nc.sbuf_tensor(name, shape, dt))

        def sem(name):
            return ctx.enter_context(nc.semaphore(name))

        raw = sb("raw", [P, RAW, SLAB])
        wh = sb("wh", [P, WH, SLAB], F32R)
        wl = sb("wl", [P, WL, SLAB], F32R)
        act_h = sb("act_h", [P, KD, T], F32R)
        act_l = sb("act_l", [P, KD, T], F32R)
        mix_h = sb("mix_h", [P, 8, T], F32R)
        mix_l = sb("mix_l", [P, 8, T], F32R)
        reg_x = sb("reg_x", [P, KD * T])
        reg_qkf = sb("reg_qkf", [P, 3 * 8 * T])
        reg_g = sb("reg_g", [P, 8, T])
        reg_v = sb("reg_v", [P, 3072])
        reg_a = sb("reg_a", [P, 3072])
        reg_t = sb("reg_t", [P, 2016])
        small = sb("small", [P, 264])
        masks = sb("masks", [P, len(LEVELS) * P], U8)
        gains = sb("gains", [P, 2, KD])
        head_g = sb("head_g", [P, 4])
        sinks = sb("sinks", [P, BH])
        lbs = sb("lbs", [P, 4, AH])
        st = sb("st", [P, 2, 5, 4])
        ones = sb("ones", [P, P])
        ident = small[:, 0:128]
        pair_win = small[:, 128:192]
        whole_win = small[:, 192:256]
        own = small[0:TS, 256:264]

        xT = reg_x[:, :].rearrange("p (k t) -> p k t", k=KD)
        xtok = reg_qkf[:, 0:NTT * D].rearrange("p (j d) -> p j d", j=NTT)
        q_a = reg_qkf[:, 0:8 * T].rearrange("p (h t) -> p h t", h=AH)
        k_a = reg_qkf[:, 8 * T:16 * T].rearrange("p (h t) -> p h t", h=AH)
        f_a = reg_qkf[:, 16 * T:24 * T].rearrange("p (h t) -> p h t", h=AH)
        tmp = reg_t[:, :].rearrange("p (n t) -> p n t", t=T)
        x_ssq = tmp[:, 5, 0:NTT]
        rms_diag = reg_t[:, 0:NTT * P].rearrange("p (j t) -> p j t", j=NTT)

        def xn(k):
            if k < 8:
                return reg_g[:, k, :]
            if k < 15:
                return reg_v[:, 1024 + T * (k - 8):1024 + T * (k - 7)]
            return tmp[:, 2, :]

        kvT = reg_v[:, 0:1152].rearrange("p (c t) -> p c t", c=4)
        k_both = reg_v[:, 1152:2304].rearrange("p (k t) -> p k t", k=KVH)
        v_tok = reg_v[:, 2304:3072].rearrange("p (j c) -> p j c", j=NTT)
        scores = reg_a[:, 0:2048].rearrange("p (n h s) -> p n h s", n=2, h=G)
        bias_buf = [reg_a[:, 2048:3072].rearrange("p (h s) -> p h s", h=G),
                    reg_x[:, 0:1024].rearrange("p (h s) -> p h s", h=G)]
        probs_t = reg_x[:, 1024:2048].rearrange("p (b h t) -> p b h t", b=2, h=G)
        v_cache = reg_x[:, 2048:4096].rearrange("p (b c) -> p b c", b=NB)
        k_tok = reg_x[:, 4096:4608].rearrange("p (j c) -> p j c", j=2)
        NK = WIN + TS
        s_scores = reg_a[:, 0:NB * NK].rearrange("p (b s) -> p b s", b=NB)
        s_bias_new = reg_a[:, 1280:1536].rearrange("p (b s) -> p b s", b=NB)
        k_cache = [reg_a[:, 1536:2048].rearrange("p (n c) -> p n c", n=2),
                   reg_t[:, 576:1088].rearrange("p (n c) -> p n c", n=2)]
        q_rows = reg_a[:, 2048:3072].rearrange("p (k b m) -> p k b m", k=KVH, b=NB)
        kT_cache = reg_x[:, 0:4 * NK].rearrange("p (n c s) -> p n c s", n=2, c=2)
        s_probs_t = reg_x[:, 1024:2048].rearrange("p (b m) -> p b m", b=NB)
        s_new_t = reg_t[0:TS, 576:1600].rearrange("p (b m) -> p b m", b=NB)
        s_out = reg_x[:, 640:896].rearrange("p (m t) -> p m t", m=8)
        s_bias = reg_t[:, 1600:1732]
        s_st = reg_t[:, 1732:1772].rearrange("p (n b) -> p n b", n=5)
        norm_rows = reg_t[0:32, 1152:1440]
        head_rows = mix_h[0:64, 1:6, :].rearrange("p m t -> p (m t)")[:, 0:20 * HD]
        norm_split = mix_h[0:64, 0, :]
        early = reg_a[:, 0:896]
        table = reg_a[0:33, 896:912]
        by_dist = reg_a[0:BH, 912:1296]
        sink_col = reg_a[0:BH, 1296:1297]
        masks_f = reg_v[:, 0:len(LEVELS) * P]
        v_a = reg_v[:, :].rearrange("p (j c) -> p j c", j=NTT)
        a_own = reg_a[:, 0:2048].rearrange("p (h j t) -> p h j t", h=AH, j=2)
        a_cross = reg_a[:, 2048:3072].rearrange("p (h t) -> p h t", h=AH)
        a_s = reg_t[0:TS, 1152:1408].rearrange("p (h t) -> p h t", h=AH)
        iT = tmp[:, 2:4, :]
        sig = tmp[:, 0:2, :]
        s0 = reg_x[:, 0:2048].rearrange("p (n b v) -> p n b v", n=2, b=NB)
        v_own = reg_x[0:TS, 2048:4096].rearrange("p (n b v) -> p n b v", n=2, b=NB)
        kt_s = reg_x[0:TS, 4096:4352].rearrange("p (n k) -> p n k", n=2)
        kt_p = reg_t[:, 1408:1920].rearrange("p (n j k) -> p n j k", n=2, j=2)
        st_p = reg_t[:, 576:832].rearrange("p (n v) -> p n v", n=2)
        h_rows = reg_t[0:32, 1408:1696]
        h_split = act_h[0:64, 8, :]
        h_pick = act_h[0:64, 9, 0:16]
        rstd2 = tmp[:, 6, :]

        acc = [ctx.enter_context(nc.psum_tensor(f"acc{i}", [P, 512], F32)) for i in range(4)]
        mx = ctx.enter_context(nc.psum_tensor("mx", [P, 4, 512], F32))

        x_in = [sem(f"x_in{j}") for j in range(NTT)]
        gain_in = sem("gain_in")
        consts_in = sem("consts_in")
        small_in = sem("small_in")
        early_in = sem("early_in")
        raw_in = [sem(f"raw_in{i}") for i in range(RAW)]
        high_done = sem("high_done")
        low_done = sem("low_done")
        unit_done = sem("unit_done")
        ones_set = sem("ones_set")
        dve_seq = sem("dve_seq")
        act_seq = sem("act_seq")
        xt_done = sem("xt_done")
        xt_copied = sem("xt_copied")
        ssq_zero = sem("ssq_zero")
        ssq_done = sem("ssq_done")
        diag_made = sem("diag_made")
        rms_spread = sem("rms_spread")
        rms_copied = sem("rms_copied")
        ms_done = sem("ms_done")
        rt_done = sem("rt_done")
        xn_done = sem("xn_done")
        acth_done = sem("acth_done")
        actl_done = sem("actl_done")
        spilled = sem("spilled")
        reloaded = sem("reloaded")
        qkv_done = sem("qkv_done")
        qk_sq = sem("qk_sq")
        qk_ssq = sem("qk_ssq")
        rows_spread = sem("rows_spread")
        rows_done = sem("rows_done")
        rows_high = sem("rows_high")
        rows_low = sem("rows_low")
        qk_bc = sem("qk_bc")
        qk_normed = sem("qk_normed")
        k_copied = sem("k_copied")
        vk_t = sem("vk_t")
        vk_tok = sem("vk_tok")
        lut_done = sem("lut_done")
        lut_copied = sem("lut_copied")
        masks_done = sem("masks_done")
        lut_out = sem("lut_out")
        bias_in = [sem("bias_in0"), sem("bias_in1")]
        sc_done = sem("sc_done")
        sc_biased = sem("sc_biased")
        sc_max = sem("sc_max")
        sc_exp = sem("sc_exp")
        sc_inv = sem("sc_inv")
        sc_probs = sem("sc_probs")
        pt_done = sem("pt_done")
        pt_copied = sem("pt_copied")
        pv_done = sem("pv_done")
        mixh_done = sem("mixh_done")
        mixl_done = sem("mixl_done")
        vc_in = sem("vc_in")
        kc_in = [sem("kc_in0"), sem("kc_in1")]
        kc_t = sem("kc_t")
        kc_copied = sem("kc_copied")
        kn_copied = sem("kn_copied")
        qr_zero = sem("qr_zero")
        sb_new = sem("sb_new")
        qr_done = sem("qr_done")
        ss_done = sem("ss_done")
        ss_biased = sem("ss_biased")
        ss_max = sem("ss_max")
        ss_exp = sem("ss_exp")
        ss_probs = sem("ss_probs")
        sp_t = sem("sp_t")
        sp_copied = sem("sp_copied")
        so_done = sem("so_done")
        so_copied = sem("so_copied")
        lb_sub = sem("lb_sub")
        lb_exp = sem("lb_exp")
        f_sig = sem("f_sig")
        k_made = sem("k_made")
        q_sig = sem("q_sig")
        q_made = sem("q_made")
        i_copied = sem("i_copied")
        g_sig = sem("g_sig")
        g_made = sem("g_made")
        v_t = sem("v_t")
        v_tokd = sem("v_tokd")
        lv_done = sem("lv_done")
        lv_kept = sem("lv_kept")
        lv_next = sem("lv_next")
        at_zero = sem("at_zero")
        s0_in = [sem("s0_in0"), sem("s0_in1")]
        kt_copied = sem("kt_copied")
        v_owned = sem("v_owned")
        sm_o = sem("sm_o")
        sm_oc = sem("sm_oc")
        sm_st = sem("sm_st")
        s0_new = sem("s0_new")
        s0_out = [sem("s0_out0"), sem("s0_out1")]
        po_done = sem("po_done")
        po_copied = sem("po_copied")
        ktp_done = sem("ktp_done")
        ktp_copied = sem("ktp_copied")
        ps_done = sem("ps_done")
        ps_copied = sem("ps_copied")
        ps_out = sem("ps_out")
        h_sq = sem("h_sq")
        h_ssq = sem("h_ssq")
        h_rowsd = sem("h_rowsd")
        h_picked = sem("h_picked")
        h_rows_high = sem("h_rows_high")
        h_rows_low = sem("h_rows_low")
        h_bc = sem("h_bc")
        h_normed = sem("h_normed")
        h_gated = sem("h_gated")
        hh_done = sem("hh_done")
        hl_done = sem("hl_done")
        x_added = sem("x_added")
        sq2_done = sem("sq2_done")
        ssq2_done = sem("ssq2_done")
        xgh_done = sem("xgh_done")
        xgl_done = sem("xgl_done")
        rstd2_done = sem("rstd2_done")
        gate_scaled = sem("gate_scaled")
        gate_silu = sem("gate_silu")
        gate_ready = sem("gate_ready")
        inner_done = sem("inner_done")
        innerh_done = sem("innerh_done")
        innerl_done = sem("innerl_done")
        down_added = sem("down_added")
        yt_done = sem("yt_done")
        yt_copied_a = sem("yt_copied_a")
        yt_copied_v = sem("yt_copied_v")
        y_out = sem("y_out")
        outs = sem("outs")
        n_outs = [0]

        def out_dma(eng, dst, src):
            eng.dma_start(dst, src).then_inc(outs, 16)
            n_outs[0] += 1

        block = ctx.enter_context(nc.Block())

        def units_through(s):
            return s + 1 if s < S_O else U_O + 2 * (s - S_O + 1)

        def units_ffn(c, i, down):
            if down:
                return U_FFN + 8 * (c + 2 if isinstance(c, int) and c < NCH - 1 or not isinstance(c, int) else NCH) \
                    + 16 * c + 4 * (i + 1)
            if isinstance(c, int) and c < 2:
                return U_FFN + 8 * c + i + 1
            return U_FFN + 8 * c + 16 * (c - 1) + i + 1

        def gu_slab(c):
            return S_FFN + 8 * c if isinstance(c, int) and c < 2 else S_FFN + 8 * c + 4 * (c - 1)

        def dn_slab(c):
            return S_FFN + 8 * NCH + 4 * c if isinstance(c, int) and c == NCH - 1 else S_FFN + 8 * (c + 2) + 4 * c

        def ffn_walk(eng, gate_up, down):
            gate_up(0, 0)
            gate_up(1, 1)
            down(0, 0)
            with eng.Fori(0, (NCH - 3) // 2) as j:
                gate_up(2 * j + 2, 2)
                down(2 * j + 1, 1)
                gate_up(2 * j + 3, 3)
                down(2 * j + 2, 2)
            gate_up(NCH - 1, NCH - 1)
            down(NCH - 2, NCH - 2)
            down(NCH - 1, NCH - 1)

        @block.sync
        def _(sp):
            sp.dma_start(xtok[0:TS, 2, :], x_sample.rearrange("b l d -> (b l) d")).then_inc(x_in[2], 16)
            for j in range(2):
                sp.dma_start(xtok[:, j, :], x_prompt[0, P * j:P * j + P, :]).then_inc(x_in[j], 16)

            def load(s, slot, src, k):
                if not (isinstance(s, int) and s < RAW):
                    sp.wait_ge(low_done, s - RAW + 1)
                sp.dma_start(raw[:, slot % RAW, :].rearrange("p (k c) -> p k c", k=k), src)\
                    .then_inc(raw_in[slot % RAW], 16)

            for s in range(S_O):
                load(s, s, win_v[:, :, IN_COLS[s]:IN_COLS[s] + P], KD)
            for s in range(S_O, S_FFN):
                half, m = divmod(s - S_O, 8)
                rows = slice(8, 16) if half == 0 else slice(0, 8)
                load(s, s, wout_v[:, rows, 2 * P * m:2 * P * (m + 1)], 8)

            def gate_up(c, cs):
                for i in range(GU):
                    src = (wg_v if i % 2 == 0 else wu_v)[:, :, bass.ds(c * (FC * P) + P * (i // 2), P)]
                    load(gu_slab(c) + i, gu_slab(cs) + i, src, KD)

            def down(c, cs):
                for i in range(DN):
                    src = w_down[bass.ds(c * (FC * P), FC * P), 512 * i:512 * i + 512]\
                        .rearrange("(k p) n -> p k n", p=P)
                    load(dn_slab(c) + i, dn_slab(cs) + i, src, FC)

            ffn_walk(sp, gate_up, down)
            for q in range(4):
                cols = slice(512 * q, 512 * q + 512)
                sp.wait_ge(yt_copied_a, 2 * q + 2)
                sp.wait_ge(yt_copied_v, q + 1)
                for j in range(2):
                    sp.dma_start(y_prompt[0, P * j:P * j + P, cols], xtok[:, j, cols]).then_inc(y_out, 16)
                sp.dma_start(y_sample.rearrange("b l d -> (b l) d")[:, cols], xtok[0:TS, 2, cols]).then_inc(y_out, 16)
            sp.wait_ge(y_out, 16 * 12)

        @block.gpsimd
        def _(pool):
            nc.gpsimd.memset(ones[:], 1.0).then_inc(ones_set, 1)
            with nc.allow_non_contiguous_dma(reason="gains, a few KB"):
                pool.dma_start(gains[:, 0, :], norm_mix.rearrange("o (k p) -> p (o k)", p=P)).then_inc(gain_in, 16)
            pool.dma_start(masks_f, c_masks).then_inc(early_in, 16)
            with nc.allow_non_contiguous_dma(reason="gains, a few KB"):
                pool.dma_start(gains[:, 1, :], norm_ffn.rearrange("o (k p) -> p (o k)", p=P)).then_inc(consts_in, 16)
                for half in range(2):
                    rows = slice(HD * half, HD * half + HD)
                    pool.dma_start(head_g[rows, 0:1], q_norm.rearrange("o d -> d o")).then_inc(consts_in, 16)
                    pool.dma_start(head_g[rows, 1:2], k_norm.rearrange("o d -> d o")).then_inc(consts_in, 16)
                pool.dma_start(head_g[:, 2:3], hgrn_norm.rearrange("o d -> d o")).then_inc(consts_in, 16)
                pool.dma_start(lbs[:, 0, :], lower_bounds.rearrange("o (h p) -> p (o h)", p=P)).then_inc(consts_in, 16)
                pool.dma_start(sinks[:, :], bass.AP(attn_sinks.tensor, 0, [[0, P], [1, BH]])).then_inc(consts_in, 16)
                pool.dma_start(early, c_early).then_inc(early_in, 16)
                pool.dma_start(table[0:N_BUCKETS, :], rel_bias_table).then_inc(early_in, 16)
                pool.dma_start(sink_col, attn_sinks.rearrange("o h -> h o")).then_inc(early_in, 16)
            pool.wait_ge(ones_set, 1)
            nc.gpsimd.memset(table[32:33, :], NEG).then_inc(at_zero, 1)
            pool.wait_ge(at_zero, 1)
            pool.wait_ge(xt_copied, KD)
            pool.dma_start(x_spill, reg_x[:, :]).then_inc(spilled, 16)
            pool.wait_ge(small_in, 16)
            for n in range(2):
                rows = slice(32 * n, 32 * n + 32)
                nc.gpsimd.tensor_copy(head_rows[rows].rearrange("p (c d) -> p c d", d=HD),
                                      ident[rows, 32 * n:32 * n + 20].unsqueeze(2).broadcast_to([32, 20, HD]))\
                    .then_inc(rows_spread, 1)
            pool.wait_ge(lut_copied, 1)
            for h in range(BH):
                pool.dma_start(bias_rows[h:h + 1], by_dist[h:h + 1, :].unsqueeze(1).broadcast_to([1, P, 384]))\
                    .then_inc(lut_out, 16)
            pool.wait_ge(lut_out, 16 * BH)

            def load_bias(k):
                for par in range(2):
                    for gg in range(2):
                        head = G * k + 2 * gg + par
                        src = bass.AP(bias_rows.tensor, head * P * 384 + 127, [[383, P], [1, 2 * WIN]])
                        pool.dma_start(bias_buf[k % 2][:, 2 * par + gg, :], src).then_inc(bias_in[k % 2], 16)

            load_bias(0)
            pool.wait_ge(spilled, 16)
            load_bias(1)
            pool.dma_start(v_cache[:, :, :], cache_v[0].rearrange("b s k d -> s b (k d)")).then_inc(vc_in, 16)
            out_dma(pool, sample_k[0, :, 0:WIN - LB].rearrange("b s k d -> b (s k d)"),
                    cache_k[0, :, LB:WIN].rearrange("b s k d -> b (s k d)"))
            out_dma(pool, sample_v[0, :, 0:WIN - LB].rearrange("b s k d -> b (s k d)"),
                    cache_v[0, :, LB:WIN].rearrange("b s k d -> b (s k d)"))

            for n in range(2 * KVH):
                k, j = divmod(n, 2)
                pool.wait_ge(sc_exp, n + 1)
                pool.wait_ge(sc_inv, n + 1)
                cols = slice(0, 2 * WIN) if j else slice(WIN, 2 * WIN)
                width = 2 * WIN if j else WIN
                sc = scores[:, n % 2, :, cols]
                nc.gpsimd.tensor_tensor(sc, sc, st[:, n % 2, 4, :].unsqueeze(2).broadcast_to([P, G, width]),
                                        ALU.mult).then_inc(sc_probs, 1)
                if j == 1 and k + 2 < KVH:
                    pool.wait_ge(sc_biased, n + 1)
                    load_bias(k + 2)
                if n == 0:
                    pool.wait_ge(vk_tok, 3)
                rows = slice(LB * n, LB * n + LB)
                out_dma(pool, sample_k[0, n, WIN - LB:WIN].rearrange("s k d -> s (k d)"), k_tok[rows, 1, :])
                out_dma(pool, sample_v[0, n, WIN - LB:WIN].rearrange("s k d -> s (k d)"), v_tok[rows, 2, :])
                if n == 2:
                    out_dma(pool, prompt_k[0, 0].rearrange("s k d -> s (k d)"), k_tok[:, 0, :])
                if n == 4:
                    out_dma(pool, prompt_v[0, 0].rearrange("s k d -> s (k d)"), v_tok[:, 1, :])
            pool.wait_ge(sc_biased, 2 * KVH)
            pool.wait_ge(pt_done, 2 * KVH)
            nc.gpsimd.memset(q_rows, 0.0).then_inc(qr_zero, 1)
            nc.gpsimd.memset(s_bias_new, NEG).then_inc(qr_zero, 1)
            for i in range(NB // 2):
                if i >= 2:
                    pool.wait_ge(kc_t, i - 1)
                for n in range(2):
                    pool.dma_start(k_cache[i % 2][:, n, :], cache_k[0, 2 * i + n].rearrange("s k d -> s (k d)"))\
                        .then_inc(kc_in[i % 2], 16)
            pool.wait_ge(so_copied, 2)
            nc.gpsimd.memset(reg_a[:, :], 0.0).then_inc(at_zero, 1)
            nc.gpsimd.memset(a_s, 0.0).then_inc(at_zero, 1)

            def load_state(h):
                pool.dma_start(s0[:, h % 2], state_hgrn[0, :, h].rearrange("b k v -> k b v")).then_inc(s0_in[h % 2], 16)

            pool.wait_ge(mixl_done, 2 * KVH + 1)
            pool.wait_ge(outs, 16 * TOKEN_OUTS)
            load_state(0)
            load_state(1)
            for h in range(AH):
                pool.wait_ge(v_tokd, h + 1)
                if h >= 2:
                    pool.wait_ge(sm_st, 2 * (h - 1))
                nc.gpsimd.tensor_tensor(
                    v_own[:, h % 2], v_a[0:TS, 2, P * h:P * h + P].unsqueeze(1).broadcast_to([TS, NB, P]),
                    own.unsqueeze(2).broadcast_to([TS, NB, P]), ALU.mult).then_inc(v_owned, 1)
                if h >= 1:
                    pool.wait_ge(s0_new, 2 * h)
                    pool.dma_start(sample_state[0, :, h - 1].rearrange("b k v -> k b v"), s0[:, (h - 1) % 2])\
                        .then_inc(s0_out[(h - 1) % 2], 16)
                    if h + 1 < AH:
                        pool.wait_ge(s0_out[(h - 1) % 2], 16 * ((h - 1) // 2 + 1))
                        load_state(h + 1)
            pool.wait_ge(s0_new, 2 * AH)
            pool.dma_start(sample_state[0, :, AH - 1].rearrange("b k v -> k b v"), s0[:, (AH - 1) % 2])\
                .then_inc(s0_out[(AH - 1) % 2], 16)
            for n in range(2):
                pool.wait_ge(s0_out[n], 16 * AH // 2)
            pool.dma_start(reg_x[:, :], x_spill).then_inc(reloaded, 16)
            for i in range(AH // 2):
                pool.wait_ge(ps_copied, i + 1)
                pool.dma_start(prompt_state[0, 0, 2 * i:2 * i + 2].rearrange("h k v -> k h v"), st_p)\
                    .then_inc(ps_out, 16)
            pool.wait_ge(ps_out, 16 * AH // 2)
            pool.wait_ge(h_ssq, AH)
            for m in range(KD):
                pool.wait_ge(x_added, 17 + m)
                if m >= 2:
                    pool.wait_ge(sq2_done, 2 * m - 1)
                nc.gpsimd.tensor_tensor(tmp[:, 1 if m else 0, :], xT[:, m, :], xT[:, m, :], ALU.mult)\
                    .then_inc(sq2_done, 1)
                if m:
                    pool.wait_ge(sq2_done, 2 * m)
                    nc.gpsimd.tensor_tensor(tmp[:, 0, :], tmp[:, 0, :], tmp[:, 1, :], ALU.add).then_inc(sq2_done, 1)
            pool.wait_ge(outs, 16 * n_outs[0])

        @block.scalar
        def _(act):
            seq = [0]

            def link(ins):
                seq[0] += 1
                ins.then_inc(act_seq, 1)
                act.wait_ge(act_seq, seq[0])

            def high(s, slot, units):
                act.wait_ge(raw_in[slot % RAW], 16 * ((s - slot % RAW) // RAW + 1) if isinstance(s, int) else
                            raw_count(s, slot))
                if units is not None:
                    act.wait_ge(unit_done, units)
                nc.scalar.activation(wh[:, slot % WH, :], raw[:, slot % RAW, :], ACT.Copy).then_inc(high_done, 1)

            def x_squares():
                act.wait_ge(ssq_zero, 1)
                for n, j in enumerate((2, 0, 1)):
                    rows = P if j < 2 else TS
                    if n:
                        act.wait_ge(ssq_done, n)
                    act.wait_ge(x_in[j], 16)
                    nc.scalar.activation(reg_g[0:rows, :, :].rearrange("p h t -> p (h t)")[:, 0:D], xtok[0:rows, j, :],
                                         ACT.Square, accum_out=x_ssq[0:rows, j:j + 1]).then_inc(ssq_done, 1)

            def x_tile(k):
                act.wait_ge(xt_done, k + 1)
                nc.scalar.activation(xT[:, k, :], mx[:, k % 4, 0:T], ACT.Copy).then_inc(xt_copied, 1)

            def root(n, rows):
                act.wait_ge(ms_done, n)
                nc.scalar.activation(rows, rows, ACT.Sqrt).then_inc(rt_done, 1)

            def x_high(k):
                act.wait_ge(xn_done, k + 1)
                nc.scalar.activation(act_h[:, k, :], xn(k), ACT.Copy).then_inc(acth_done, 1)

            def lower_bound():
                act.wait_ge(lb_sub, 1)
                nc.scalar.activation(lbs[:, 2, :], lbs[:, 1, :], ACT.Exp).then_inc(lb_exp, 1)

            def evacuate(s):
                act.wait_ge(unit_done, s + 1)
                ps = acc[s % 4][:, 0:T]
                if s < S_F:
                    if s < 8:
                        dst = reg_g[:, s, :]
                    else:
                        act.wait_ge(masks_done, 1)
                        dst = kvT[:, s - 8, :]
                    if s < 10:
                        if s >= 2:
                            act.wait_ge(qk_ssq, s - 1)
                        nc.scalar.activation(tmp[:, s % 2, :], ps, ACT.Square).then_inc(qk_sq, 1)
                    nc.scalar.activation(dst, ps, ACT.Copy).then_inc(qkv_done, 1)
                elif s < S_Q:
                    h = s - S_F
                    nc.scalar.activation(f_a[:, h, :], ps, ACT.Sigmoid)
                    nc.scalar.activation(k_a[:, h, :], ps, ACT.Sigmoid, scale=-1.0).then_inc(f_sig, 1)
                elif s < S_I:
                    h = s - S_Q
                    if h >= 2:
                        act.wait_ge(q_made, h - 1)
                    nc.scalar.activation(sig[:, h % 2, :], ps, ACT.Sigmoid).then_inc(q_sig, 1)
                elif s < S_G:
                    h = s - S_I
                    if h == 0:
                        act.wait_ge(so_done, 1)
                    if h >= 2:
                        act.wait_ge(v_t, h - 1)
                    nc.scalar.activation(iT[:, h % 2, :], ps, ACT.Copy).then_inc(i_copied, 1)
                elif s < S_O:
                    h = s - S_G
                    if h >= 2:
                        act.wait_ge(g_made, h - 1)
                    nc.scalar.activation(sig[:, h % 2, :], ps, ACT.Sigmoid).then_inc(g_sig, 1)

            def k_halves():
                act.wait_ge(qk_normed, 2)
                for k in range(KVH):
                    src = kvT[HD * (k % 2):HD * (k % 2) + HD, k // 2, :]
                    for half in range(2):
                        nc.scalar.activation(k_both[HD * half:HD * half + HD, k, :], src, ACT.Copy)\
                            .then_inc(k_copied, 1)

            def token_major():
                act.wait_ge(vk_t, 1)
                nc.scalar.activation(v_tok[:, 0:2, :], mx[:, 0, :].rearrange("p (j c) -> p j c", j=2), ACT.Copy)\
                    .then_inc(vk_tok, 1)
                act.wait_ge(vk_t, 2)
                act.wait_ge(spilled, 16)
                nc.scalar.activation(k_tok[:, 0, :], mx[:, 2, 0:256], ACT.Copy)
                nc.scalar.activation(v_tok[0:TS, 2, :], mx[0:TS, 1, 0:256], ACT.Copy).then_inc(vk_tok, 1)
                nc.scalar.activation(k_tok[0:TS, 1, :], mx[0:TS, 1, 256:512], ACT.Copy).then_inc(vk_tok, 1)

            def exps(n):
                j = n % 2
                cols = slice(0, 2 * WIN) if j else slice(WIN, 2 * WIN)
                act.wait_ge(sc_max, n + 1)
                nc.scalar.activation(st[:, n % 2, 2, :], st[:, n % 2, 2, :], ACT.Exp)
                for h in range(G):
                    sc = scores[:, n % 2, h, cols]
                    ins = nc.scalar.activation(sc, sc, ACT.Exp, bias=st[:, n % 2, 1, h:h + 1],
                                               accum_out=st[:, n % 2, 3, h:h + 1])
                ins.then_inc(sc_exp, 1)

            def probs_copy(n):
                j = n % 2
                act.wait_ge(pt_done, n + 1)
                if n >= 1:
                    act.wait_ge(pv_done, n)
                for blk in range(1 - j, 2):
                    ins = nc.scalar.activation(probs_t[:, blk], mx[:, 2 + blk, :].rearrange("p (h t) -> p h t", h=G),
                                               ACT.Copy)
                ins.then_inc(pt_copied, 1)

            def out_high(n):
                k, j = divmod(n, 2)
                act.wait_ge(pv_done, n + 1)
                nc.scalar.activation(mix_h[:, 2 * k:2 * k + 2, P * j:P * j + P],
                                     mx[:, 2, 0:256].rearrange("p (m t) -> p m t", m=2), ACT.Copy).then_inc(mixh_done, 1)

            def q_to_rows():
                act.wait_ge(qr_zero, 2)
                for k in range(KVH):
                    for g in range(G):
                        src = reg_g[HD * (g % 2):HD * (g % 2) + HD, 2 * k + g // 2, TP:T]
                        dst = q_rows[HD * (k % 2):HD * (k % 2) + HD, k, :, LB * g:LB * g + LB]
                        nc.scalar.activation(dst, src.rearrange("p (b l) -> p b l", b=NB), ACT.Copy)\
                            .then_inc(qr_done, 1)
                act.wait_ge(sc_biased, 2 * KVH)
                for n in range(2):
                    nc.scalar.activation(kT_cache[:, n, :, WIN:NK], kvT[:, 0:2, TP:T], ACT.Copy).then_inc(kn_copied, 1)

            def s_exps():
                act.wait_ge(ss_max, 1)
                nc.scalar.activation(s_st[:, 2, :], s_st[:, 2, :], ACT.Exp)
                for b in range(NB):
                    ins = nc.scalar.activation(s_scores[:, b, :], s_scores[:, b, :], ACT.Exp,
                                               bias=s_st[:, 1, b:b + 1], accum_out=s_st[:, 3, b:b + 1])
                ins.then_inc(ss_exp, 1)

            def s_probs_copy(n):
                act.wait_ge(sp_t, n + 1)
                nc.scalar.activation(s_probs_t[:, 4 * n:4 * n + 4, :],
                                     mx[:, 2 * n, :].rearrange("p (b m) -> p b m", b=4), ACT.Copy)
                nc.scalar.activation(s_new_t[:, 4 * n:4 * n + 4, :],
                                     mx[0:TS, 2 * n + 1, :].rearrange("p (b m) -> p b m", b=4), ACT.Copy)\
                    .then_inc(sp_copied, 1)

            def s_out_copy():
                act.wait_ge(so_done, 1)
                src = mx[0:HD, 0, :].rearrange("p (k b m) -> p k b m", k=KVH, b=NB)
                dst = s_out.rearrange("p (k m) (b l) -> p k m b l", k=KVH, b=NB)
                for g in range(G):
                    ins = nc.scalar.activation(dst[HD * (g % 2):HD * (g % 2) + HD, :, g // 2],
                                               src[:, :, :, LB * g:LB * g + LB], ACT.Copy)
                ins.then_inc(so_copied, 1)
                act.wait_ge(so_copied, 1)
                nc.scalar.activation(mix_h[:, :, TP:T], s_out, ACT.Copy).then_inc(so_copied, 1)

            def v_copy(h):
                if h == 0:
                    act.wait_ge(outs, 16 * TOKEN_OUTS)
                act.wait_ge(v_t, h + 1)
                nc.scalar.activation(v_a[:, 0:2, P * h:P * h + P],
                                     mx[:, 0, 0:256].rearrange("p (j c) -> p j c", j=2), ACT.Copy)
                nc.scalar.activation(v_a[0:TS, 2, P * h:P * h + P], mx[0:TS, 0, 256:384], ACT.Copy)\
                    .then_inc(v_tokd, 1)

            def sampled_copies(h):
                act.wait_ge(sm_o, h + 1)
                if h >= 2:
                    act.wait_ge(sm_st, 2 * (h - 1))
                nc.scalar.activation(kt_s[:, h % 2, :], mx[0:TS, 1, 128:256], ACT.Copy).then_inc(kt_copied, 1)
                nc.scalar.activation(q_a[:, h, TP:T], mx[:, 1, 0:TS], ACT.Copy).then_inc(sm_oc, 1)

            def prompt_out_copy(h):
                act.wait_ge(po_done, h + 1)
                nc.scalar.activation(q_a[:, h, 0:TP], mx[:, h % 2, 0:TP], ACT.Copy).then_inc(po_copied, 1)

            def prompt_state_copies(i):
                act.wait_ge(ktp_done, i + 1)
                nc.scalar.activation(kt_p, mx[:, 2, :].rearrange("p (n j k) -> p n j k", n=2, j=2), ACT.Copy)\
                    .then_inc(ktp_copied, 1)
                act.wait_ge(ps_done, i + 1)
                if i:
                    act.wait_ge(ps_out, 16 * i)
                nc.scalar.activation(st_p, mx[:, 3, 0:256].rearrange("p (n v) -> p n v", n=2), ACT.Copy)\
                    .then_inc(ps_copied, 1)

            def h_squares(heads):
                act.wait_ge(g_made, AH)
                act.wait_ge(po_copied, AH)
                act.wait_ge(sm_oc, AH)
                for h in heads:
                    if h >= 2:
                        act.wait_ge(h_ssq, h - 1)
                    nc.scalar.activation(sig[:, h % 2, :], q_a[:, h, :], ACT.Square).then_inc(h_sq, 1)

            def h_high(heads):
                for h in heads:
                    act.wait_ge(h_gated, h + 1)
                    nc.scalar.activation(act_h[:, h, :], q_a[:, h, :], ACT.Copy).then_inc(hh_done, 1)

            def x2_high(m):
                act.wait_ge(x_added, 17 + m)
                if m == 8:
                    act.wait_ge(unit_done, U_FFN)
                nc.scalar.activation(act_h[:, x2_place(m), :], xT[:, m, :], ACT.Copy, scale=gains[:, 1, m:m + 1])\
                    .then_inc(xgh_done, 1)

            def raw_count(s, slot):
                return (s - slot % RAW) * 16 // RAW + 16

            act.dma_start(small[:, :], c_small).then_inc(small_in, 16)
            x_squares()
            for k in range(4):
                x_tile(k)
            root(1, x_ssq)
            for k in range(4, 8):
                x_tile(k)
            high(0, 0, None)
            for k in range(KD):
                if k < KD - 8:
                    x_tile(k + 8)
                x_high(k)
            high(1, 1, None)
            high(2, 2, None)
            for s in range(S_FFN):
                if 0 <= s - S_AT < 8:
                    high(s - 1 + WH, s - 1 + WH, units_through(s - 1))
                if 0 <= s - S_AT - 2 < 8:
                    out_high(s - S_AT - 2)
                if 0 <= s - S_AT < 8:
                    exps(s - S_AT)
                    evacuate(s - 1)
                if 0 <= s - S_AT - 1 < 8:
                    probs_copy(s - S_AT - 1)
                if s == S_LB:
                    lower_bound()
                if s == S_QKN - 1:
                    root(2, norm_rows)
                    act.wait_ge(rows_done, 1)
                    nc.scalar.activation(norm_split[0:32], norm_rows, ACT.Copy).then_inc(rows_high, 1)
                if s == S_QKN:
                    k_halves()
                if s == S_QKN + 1:
                    token_major()
                if s == S_SA - 1:
                    q_to_rows()
                if s == S_SA + 2:
                    s_exps()
                if s == S_SA + 4:
                    s_probs_copy(0)
                    s_probs_copy(1)
                    s_out_copy()
                if 0 <= s - S_PO < 4:
                    prompt_out_copy(2 * (s - S_PO))
                    prompt_out_copy(2 * (s - S_PO) + 1)
                if 0 <= s - S_VT < AH:
                    v_copy(s - S_VT)
                if 0 <= s - S_SM < AH:
                    sampled_copies(s - S_SM)
                if 0 <= s - S_PS < 4:
                    prompt_state_copies(s - S_PS)
                if s == S_HN:
                    h_squares(range(2, 6))
                if s == S_HN + 1:
                    h_squares(range(6, 8))
                    act.wait_ge(unit_done, S_O)
                    for n in range(2):
                        rows = slice(32 * n, 32 * n + 32)
                        nc.scalar.activation(h_pick[rows], ident[rows, 32 * n:32 * n + 16], ACT.Copy)\
                            .then_inc(h_picked, 1)
                    root(3, h_rows)
                    act.wait_ge(h_rowsd, 1)
                    nc.scalar.activation(h_split[0:32], h_rows, ACT.Copy).then_inc(h_rows_high, 1)
                if s in (S_HN + 2, S_HN + 3):
                    h_high(range(4 * (s - S_HN - 2), 4 * (s - S_HN - 1)))
                if S_AT <= s + 1 < S_AT + 8:
                    continue
                if s < S_O:
                    evacuate(s)
                if s == S_HN - 1:
                    h_squares(range(0, 2))
                if s >= S_FFN - 4:
                    for m in (2 * (s - S_FFN + 4), 2 * (s - S_FFN + 4) + 1):
                        x2_high(m)
                if s < S_FFN - 1:
                    high(s + WH, s + WH, units_through(s))
            for m in range(8, KD):
                x2_high(m)
            high(S_FFN - 1 + WH, S_FFN - 1 + WH, U_FFN)
            root(4, rstd2)

            def gate_up(c, cs):
                for i in range(GU):
                    t, up = divmod(i, 2)
                    n = c * FC + t
                    if not up:
                        act.wait_ge(gate_scaled, n + 1)
                        nc.scalar.activation(tmp[:, 2 + t % 2, :], tmp[:, t % 2, :], ACT.Silu).then_inc(gate_silu, 1)
                    else:
                        act.wait_ge(inner_done, n + 1)
                        nc.scalar.activation(mix_h[:, FC * (cs % 2) + t, :], tmp[:, 4 + t % 2, :], ACT.Copy)\
                            .then_inc(innerh_done, 1)
                    ahead(gu_slab(c) + i, gu_slab(cs) + i, units_ffn(c, i, False))

            def ahead(s, slot, units):
                if isinstance(s, int) and s + WH >= N_SLABS:
                    return
                high(s + WH, slot + WH, units)

            def down(c, cs):
                for i in range(DN):
                    ahead(dn_slab(c) + i, dn_slab(cs) + i, units_ffn(c, i, True))

            def y_copies(q):
                act.wait_ge(yt_done, q + 1)
                for j in (0, 2):
                    rows = P if j < 2 else TS
                    nc.scalar.activation(xtok[0:rows, j, 512 * q:512 * q + 512], mx[0:rows, j, :], ACT.Copy)\
                        .then_inc(yt_copied_a, 1)

            ffn_walk(act, gate_up, down)
            for q in range(4):
                y_copies(q)

        @block.vector
        def _(dve):
            seq = [0]

            def link(ins):
                seq[0] += 1
                ins.then_inc(dve_seq, 1)
                dve.wait_ge(dve_seq, seq[0])

            def low(s, slot, units):
                dve.wait_ge(high_done, s + 1)
                if units is not None:
                    dve.wait_ge(unit_done, units)
                nc.vector.tensor_tensor(wl[:, slot % WL, :], raw[:, slot % RAW, :], wh[:, slot % WH, :].bitcast(F32),
                                        ALU.subtract).then_inc(low_done, 1)

            def mean_square(rows, ps, width, n):
                nc.vector.tensor_scalar(rows, ps, 1.0 / width, EPS, ALU.mult, ALU.add).then_inc(ms_done, 1)
                dve.wait_ge(rt_done, n)

            def norm1():
                nc.vector.memset(x_ssq, 0.0).then_inc(ssq_zero, 1)
                dve.wait_ge(ssq_done, NTT)
                mean_square(x_ssq, x_ssq, D, 1)
                link(nc.vector.reciprocal(x_ssq, x_ssq))
                dve.wait_ge(small_in, 16)
                for j in range(NTT):
                    nc.vector.tensor_scalar(rms_diag[:, j, :], ident, x_ssq[:, j:j + 1], None, ALU.mult)\
                        .then_inc(diag_made, 1)
                dve.wait_ge(rms_spread, 1)
                nc.vector.tensor_copy(tmp[:, 6, :], acc[0][:, 0:T]).then_inc(rms_copied, 1)
                dve.wait_ge(rms_copied, 1)
                dve.wait_ge(gain_in, 16)
                for k in range(KD):
                    dve.wait_ge(xt_copied, k + 1)
                    nc.vector.scalar_tensor_tensor(out=xn(k), in0=xT[:, k, :], scalar=gains[:, 0, k:k + 1],
                                                   in1=tmp[:, 6, :], op0=ALU.mult, op1=ALU.mult).then_inc(xn_done, 1)
                low(0, 0, None)
                for k in range(KD):
                    dve.wait_ge(acth_done, k + 1)
                    nc.vector.tensor_tensor(act_l[:, k, :], xn(k), act_h[:, k, :].bitcast(F32), ALU.subtract)\
                        .then_inc(actl_done, 1)

            def lower_bound():
                x, d, e, r = (lbs[:, n, :] for n in range(4))
                dve.wait_ge(consts_in, 16 * 8)
                link(nc.vector.tensor_copy(r, x))
                nc.vector.tensor_tensor(d, x, r, ALU.subtract).then_inc(lb_sub, 1)
                dve.wait_ge(lb_exp, 1)
                link(nc.vector.reciprocal(r, e))
                link(nc.vector.tensor_tensor(e, e, r, ALU.mult))
                link(nc.vector.tensor_tensor(e, e, e, ALU.subtract))
                link(nc.vector.tensor_scalar(x, e, LB_FLOOR, None, ALU.max))
                link(nc.vector.tensor_scalar(d, e, -1.0, 1.0, ALU.mult, ALU.add))

            def bias_by_distance():
                dve.wait_ge(lut_done, 1)
                nc.vector.tensor_copy(by_dist, mx[0:BH, 3, 0:384]).then_inc(lut_copied, 1)

            def bias_of_rows():
                dve.wait_ge(lut_done, 2)
                nc.vector.tensor_copy(s_bias, mx[:, 2, 0:132])
                nc.vector.tensor_copy(head_g[:, 3:4], mx[:, 2, 132:133]).then_inc(lut_copied, 1)
                link(nc.vector.tensor_scalar(head_g[:, 0:1], head_g[:, 0:1], SCALE, None, ALU.mult))
                nc.vector.tensor_copy(masks[:, :], masks_f).then_inc(masks_done, 1)

            def evacuate(s):
                ps = acc[s % 4][:, 0:T]
                if S_F <= s < S_Q:
                    h = s - S_F
                    dve.wait_ge(f_sig, h + 1)
                    nc.vector.tensor_scalar(f_a[:, h, :], f_a[:, h, :], lbs[:, 1, h:h + 1], lbs[:, 0, h:h + 1],
                                            ALU.mult, ALU.add)
                    nc.vector.tensor_scalar(k_a[:, h, :], k_a[:, h, :], lbs[:, 1, h:h + 1], None, ALU.mult)\
                        .then_inc(k_made, 1)
                elif S_Q <= s < S_I:
                    h = s - S_Q
                    dve.wait_ge(q_sig, h + 1)
                    nc.vector.tensor_tensor(q_a[:, h, :], ps, sig[:, h % 2, :], ALU.mult).then_inc(q_made, 1)
                elif S_G <= s < S_O:
                    h = s - S_G
                    dve.wait_ge(g_sig, h + 1)
                    nc.vector.tensor_tensor(reg_g[:, h, :], ps, sig[:, h % 2, :], ALU.mult).then_inc(g_made, 1)

            def qk_rows():
                dve.wait_ge(qk_ssq, 10)
                mean_square(norm_rows, mx[0:32, 0, 0:T], HD, 2)
                nc.vector.reciprocal(norm_rows, norm_rows).then_inc(rows_done, 1)
                dve.wait_ge(rows_high, 1)
                nc.vector.tensor_tensor(norm_split[32:64], norm_rows, norm_split[0:32].bitcast(F32), ALU.subtract)\
                    .then_inc(rows_low, 1)

            def qk_norm():
                for n in range(10):
                    i = KEYS_FIRST[n]
                    dst = reg_g[:, i, :] if i < 8 else kvT[:, i - 8, :]
                    g = head_g[:, 0:1] if i < 8 else head_g[:, 1:2]
                    dve.wait_ge(qk_bc, n + 1)
                    nc.vector.scalar_tensor_tensor(out=dst, in0=dst, scalar=g, in1=mx[:, (1 + n) % 4, 0:T],
                                                   op0=ALU.mult, op1=ALU.mult).then_inc(qk_normed, 1)

            def softmax_front(n):
                k, j = divmod(n, 2)
                cols = slice(0, 2 * WIN) if j else slice(WIN, 2 * WIN)
                width = 2 * WIN if j else WIN
                sc = scores[:, n % 2, :, cols]
                mneg, es = st[:, n % 2, 1, :], st[:, n % 2, 2, :]
                dve.wait_ge(sc_done, n + 1)
                dve.wait_ge(bias_in[k % 2], 64 * (k // 2 + 1))
                if n >= 2:
                    dve.wait_ge(pt_done, n - 1)
                ps = mx[:, 0:2, :].rearrange("p a (b s) -> p (a b) s", b=2)[:, :, 0:width]
                nc.vector.tensor_tensor(sc, ps, bias_buf[k % 2][:, :, cols], ALU.add).then_inc(sc_biased, 1)
                dve.wait_ge(sc_biased, n + 1)
                link(nc.vector.tensor_reduce(st[:, n % 2, 0, :], sc, AX.X, ALU.max))
                sk = sinks[:, G * k:G * k + G].rearrange("p (gg par) -> p par gg", par=2)
                mx4 = st[:, n % 2, 0, :].rearrange("p (par gg) -> p par gg", par=2)
                link(nc.vector.tensor_tensor(mx4, mx4, sk, ALU.max))
                nc.vector.tensor_tensor(es.rearrange("p (par gg) -> p par gg", par=2), sk, mx4, ALU.subtract)
                nc.vector.tensor_scalar(mneg, st[:, n % 2, 0, :], -1.0, None, ALU.mult).then_inc(sc_max, 1)

            def softmax_back(n):
                dve.wait_ge(sc_exp, n + 1)
                link(nc.vector.tensor_tensor(st[:, n % 2, 3, :], st[:, n % 2, 3, :], st[:, n % 2, 2, :], ALU.add))
                nc.vector.reciprocal(st[:, n % 2, 4, :], st[:, n % 2, 3, :]).then_inc(sc_inv, 1)

            def out_low(n):
                k, j = divmod(n, 2)
                dve.wait_ge(mixh_done, n + 1)
                nc.vector.tensor_tensor(mix_l[:, 2 * k:2 * k + 2, P * j:P * j + P],
                                        mx[:, 2, 0:256].rearrange("p (m t) -> p m t", m=2),
                                        mix_h[:, 2 * k:2 * k + 2, P * j:P * j + P].bitcast(F32),
                                        ALU.subtract).then_inc(mixl_done, 1)

            def s_bias_place():
                dve.wait_ge(qr_zero, 2)
                for b in range(NB):
                    nc.vector.tensor_copy(s_bias_new[:, b, LB * b:LB * b + LB], s_bias[:, WIN:WIN + LB])\
                        .then_inc(sb_new, 1)

            def keys_copy(i):
                dve.wait_ge(kc_t, i + 1)
                if i == 0:
                    dve.wait_ge(sc_biased, 2 * KVH)
                else:
                    dve.wait_ge(ss_done, 2 * i)
                nc.vector.tensor_copy(kT_cache[:, :, :, 0:WIN],
                                      mx[:, 3, :].rearrange("p (n c s) -> p n c s", n=2, c=2)).then_inc(kc_copied, 1)

            def s_bias_add(n):
                b0, nb = 3 * n, min(3, NB - 3 * n)
                dve.wait_ge(ss_done, b0 + nb)
                if n == 0:
                    dve.wait_ge(sb_new, NB)
                    dve.wait_ge(pt_done, 2 * KVH)
                ps = mx[:, n, 0:3 * NK].rearrange("p (b s) -> p b s", b=3)[:, 0:nb, :]
                nc.vector.tensor_tensor(s_scores[:, b0:b0 + nb, 0:WIN], ps[:, :, 0:WIN],
                                        s_bias[:, 0:WIN].unsqueeze(1).broadcast_to([P, nb, WIN]), ALU.add)
                nc.vector.tensor_tensor(s_scores[:, b0:b0 + nb, WIN:NK], ps[:, :, WIN:NK],
                                        s_bias_new[:, b0:b0 + nb, :], ALU.add).then_inc(ss_biased, 1)

            def s_softmax_front():
                dve.wait_ge(ss_biased, 3)
                link(nc.vector.tensor_reduce(s_st[:, 0, :], s_scores, AX.X, ALU.max))
                link(nc.vector.tensor_scalar(s_st[:, 0, :], s_st[:, 0, :], head_g[:, 3:4], None, ALU.max))
                nc.vector.tensor_scalar(s_st[:, 1, :], s_st[:, 0, :], -1.0, None, ALU.mult)
                nc.vector.tensor_scalar(s_st[:, 2, :], s_st[:, 0, :], -1.0, head_g[:, 3:4], ALU.mult, ALU.add)\
                    .then_inc(ss_max, 1)

            def s_softmax_back():
                dve.wait_ge(ss_exp, 1)
                link(nc.vector.tensor_tensor(s_st[:, 3, :], s_st[:, 3, :], s_st[:, 2, :], ALU.add))
                link(nc.vector.reciprocal(s_st[:, 4, :], s_st[:, 3, :]))
                nc.vector.tensor_tensor(s_scores, s_scores, s_st[:, 4, :].unsqueeze(2).broadcast_to([P, NB, NK]),
                                        ALU.mult).then_inc(ss_probs, 1)

            def s_out_low():
                dve.wait_ge(so_copied, 2)
                nc.vector.tensor_tensor(mix_l[:, :, TP:T], s_out, mix_h[:, :, TP:T].bitcast(F32), ALU.subtract)\
                    .then_inc(mixl_done, 1)

            def level_merge(lv):
                mask = masks[:, P * lv:P * lv + P]
                for b in range(4):
                    dve.wait_ge(lv_done, lv_unit(lv, b) + 1)
                    if lv == 0 and b == 0:
                        dve.wait_ge(at_zero, 3)
                    if lv:
                        dve.wait_ge(lv_kept, lv_unit(lv - 1, b) + 1)
                    own = reg_a[:, 512 * b:512 * b + 512]
                    ps = mx[:, b, :]
                    if lv:
                        own, ps = right_halves(own, LEVELS[lv]), blocks_of(ps[:, 0:256], LEVELS[lv])
                        keep = right_halves(mask, LEVELS[lv])
                    else:
                        own, ps, keep = own.unsqueeze(2), ps.unsqueeze(2), mask.unsqueeze(2)
                    own, ps = (a.rearrange("p (hj b) n -> p hj b n", hj=4) for a in (own, ps))
                    nc.vector.copy_predicated(own, keep.unsqueeze(1).broadcast_to(list(own.shape)), ps)\
                        .then_inc(lv_kept, 1)
                if lv < 3:
                    dve.wait_ge(lv_done, lv_unit(lv, 4) + 1)
                    if lv:
                        dve.wait_ge(lv_kept, lv_unit(lv - 1, 4) + 1)
                    own, ps, keep = reg_t[0:TS, 1152:1408], mx[0:TS, 0, 0:256], mask[0:TS, 0:TS]
                    if lv:
                        own, ps = right_halves(own, LEVELS[lv]), blocks_of(ps[:, 0:128], LEVELS[lv])
                        keep = right_halves(keep, LEVELS[lv])
                    else:
                        own, ps, keep = own.unsqueeze(2), ps.unsqueeze(2), keep.unsqueeze(2)
                    own, ps = (a.rearrange("p (h b) n -> p h b n", h=AH) for a in (own, ps))
                    nc.vector.copy_predicated(own, keep.unsqueeze(1).broadcast_to(list(own.shape)), ps)\
                        .then_inc(lv_kept, 1)

            def level_up(lv):
                n = LEVELS[lv]
                if lv == 0:
                    nc.vector.tensor_tensor(reg_qkf[:, 0:8 * T], reg_qkf[:, 0:8 * T], reg_qkf[:, 16 * T:24 * T],
                                            ALU.mult).then_inc(lv_next, 1)
                    return
                width = T if n < LB else TP
                def blocks(a):
                    return a[:, :, 0:width].rearrange("p h (b two n) -> p h b two n", two=2, n=n)
                nblk = width // (2 * n)
                fl, fr = blocks(f_a)[:, :, :, 0, 0:1], blocks(f_a)[:, :, :, 1, 0:1]
                q_r, k_l = blocks(q_a)[:, :, :, 1, :], blocks(k_a)[:, :, :, 0, :]
                if n == 1:
                    fb, fa = fl, fr
                else:
                    fb, fa = fl.broadcast_to([P, AH, nblk, n]), fr.broadcast_to([P, AH, nblk, n])
                nc.vector.tensor_tensor(q_r, q_r, fb, ALU.mult)
                link(nc.vector.tensor_tensor(k_l, k_l, fa, ALU.mult))
                nc.vector.tensor_tensor(fl, fl, fr, ALU.mult).then_inc(lv_next, 1)

            def next_level(lv):
                dve.wait_ge(lv_done, lv_units_through(lv))
                if lv:
                    dve.wait_ge(lv_next, lv)
                level_up(lv)

            def cross_copy():
                for b in range(2):
                    dve.wait_ge(lv_done, lv_units_through(7) + b + 1)
                    nc.vector.tensor_copy(a_cross[:, 4 * b:4 * b + 4, :],
                                          mx[:, b, :].rearrange("p (h t) -> p h t", h=4)).then_inc(lv_kept, 1)
                dve.wait_ge(lv_next, 8)
                nc.vector.tensor_tensor(k_a[:, :, 0:P], k_a[:, :, 0:P], f_a[:, :, P:P + 1].broadcast_to([P, AH, P]),
                                        ALU.mult).then_inc(lv_next, 1)

            def new_states(h):
                dve.wait_ge(s0_in[h % 2], 16 * (h // 2 + 1))
                for half in range(2):
                    dve.wait_ge(sm_st, 2 * h + half + 1)
                    for b in range(4 * half, 4 * half + 4):
                        s = s0[:, h % 2, b, :]
                        ins = nc.vector.scalar_tensor_tensor(
                            out=s, in0=s, scalar=f_a[:, h, TP + LB * b:TP + LB * b + 1],
                            in1=mx[:, 2 + half, P * (b % 4):P * (b % 4) + P], op0=ALU.mult, op1=ALU.add)
                    ins.then_inc(s0_new, 1)

            def h_norm_rows():
                dve.wait_ge(h_ssq, AH)
                dve.wait_ge(ps_done, AH // 2)
                mean_square(h_rows, mx[0:32, 0, 0:T], P, 3)
                nc.vector.reciprocal(h_rows, h_rows).then_inc(h_rowsd, 1)
                dve.wait_ge(h_rows_high, 1)
                nc.vector.tensor_tensor(h_split[32:64], h_rows, h_split[0:32].bitcast(F32), ALU.subtract)\
                    .then_inc(h_rows_low, 1)

            def h_out(heads):
                def gate(h):
                    dve.wait_ge(h_normed, h + 1)
                    nc.vector.tensor_tensor(q_a[:, h, :], q_a[:, h, :], reg_g[:, h, :], ALU.mult).then_inc(h_gated, 1)

                def lows(h):
                    dve.wait_ge(hh_done, h + 1)
                    nc.vector.tensor_tensor(act_l[:, h, :], q_a[:, h, :], act_h[:, h, :].bitcast(F32),
                                            ALU.subtract).then_inc(hl_done, 1)

                for h in heads:
                    dve.wait_ge(h_bc, h + 1)
                    nc.vector.scalar_tensor_tensor(out=q_a[:, h, :], in0=q_a[:, h, :], scalar=head_g[:, 2:3],
                                                   in1=mx[:, (1 + h) % 4, 0:T], op0=ALU.mult, op1=ALU.mult)\
                        .then_inc(h_normed, 1)
                    gate(h)
                for h in heads:
                    lows(h)

            def add_unit(u):
                m = u % 16
                if u == 0:
                    dve.wait_ge(reloaded, 16)
                if u >= 16:
                    dve.wait_ge(x_added, m + 1)
                dve.wait_ge(unit_done, U_O + u + 1)
                nc.vector.tensor_tensor(xT[:, m, :], acc[(U_O + u) % 4][:, 0:T], xT[:, m, :], ALU.add)\
                    .then_inc(x_added, 1)

            def x2_low(m):
                dve.wait_ge(xgh_done, m + 1)
                nc.vector.scalar_tensor_tensor(out=act_l[:, x2_place(m), :], in0=xT[:, m, :],
                                               scalar=gains[:, 1, m:m + 1],
                                               in1=act_h[:, x2_place(m), :].bitcast(F32),
                                               op0=ALU.mult, op1=ALU.subtract).then_inc(xgl_done, 1)

            norm1()
            low(1, 1, None)
            for s in range(S_FFN):
                if 0 <= s - S_AT < 8:
                    softmax_front(s - S_AT)
                if 0 <= s - S_AT - 2 < 8:
                    out_low(s - S_AT - 2)
                if 0 <= s - S_AT < 8:
                    low(s - 1 + WL, s - 1 + WL, units_through(s - 1))
                    softmax_back(s - S_AT)
                    evacuate(s - 1)
                if s == S_LB:
                    lower_bound()
                if s == S_QKN - 1:
                    qk_rows()
                if s == S_QKN:
                    qk_norm()
                if s == S_LUT:
                    bias_by_distance()
                if s == S_LUT + 1:
                    bias_of_rows()
                if s == S_SA - 1:
                    s_bias_place()
                if S_SA <= s <= S_SA + 1:
                    keys_copy(2 * (s - S_SA))
                    keys_copy(2 * (s - S_SA) + 1)
                if s == S_SA + 1:
                    s_bias_add(0)
                if s == S_SA + 2:
                    s_bias_add(1)
                    s_bias_add(2)
                    s_softmax_front()
                    s_softmax_back()
                if s == S_SA + 4:
                    s_out_low()
                if 0 <= s - S_SM - 1 < AH:
                    new_states(s - S_SM - 1)
                    low(s - 1 + WL, s - 1 + WL, units_through(s - 1))
                if 0 <= s - S_LV < 8:
                    level_merge(s - S_LV)
                    next_level(s - S_LV)
                if s == S_LV + 8:
                    cross_copy()
                if s == S_HN + 1:
                    h_norm_rows()
                if s in (S_HN + 2, S_HN + 3):
                    h_out(range(4 * (s - S_HN - 2), 4 * (s - S_HN - 1)))
                if S_AT <= s + 1 < S_AT + 8:
                    continue
                if s < S_O:
                    evacuate(s)
                if S_O <= s:
                    for u in (2 * (s - S_O), 2 * (s - S_O) + 1):
                        add_unit(u)
                if s >= S_FFN - 4:
                    for m in (2 * (s - S_FFN + 4), 2 * (s - S_FFN + 4) + 1):
                        x2_low(m)
                if not (S_SM <= s < S_SM + AH or s == S_FFN - 1):
                    low(s + WL, s + WL, units_through(s))
            for m in range(8, KD):
                x2_low(m)
            low(S_FFN - 1 + WL, S_FFN - 1 + WL, U_FFN)
            dve.wait_ge(ssq2_done, 1)
            mean_square(rstd2, mx[:, 0, 0:T], D, 4)
            nc.vector.reciprocal(rstd2, rstd2).then_inc(rstd2_done, 1)
            dve.wait_ge(rstd2_done, 1)

            def gate_up(c, cs):
                for i in range(GU):
                    t, up = divmod(i, 2)
                    n = c * FC + t
                    ps = acc[bank_gu(cs, i)][:, 0:T]
                    dve.wait_ge(unit_done, units_ffn(c, i, False))
                    if not up:
                        if not (isinstance(c, int) and c == 0 and t < 2):
                            dve.wait_ge(gate_silu, n - 1)
                        nc.vector.tensor_tensor(tmp[:, t % 2, :], ps, rstd2, ALU.mult).then_inc(gate_scaled, 1)
                        dve.wait_ge(gate_silu, n + 1)
                        nc.vector.tensor_tensor(tmp[:, 2 + t % 2, :], tmp[:, 2 + t % 2, :], rstd2, ALU.mult)\
                            .then_inc(gate_ready, 1)
                    else:
                        dve.wait_ge(gate_ready, n + 1)
                        if not (isinstance(c, int) and c == 0 and t < 2):
                            dve.wait_ge(innerl_done, n - 1)
                        nc.vector.tensor_tensor(tmp[:, 4 + t % 2, :], ps, tmp[:, 2 + t % 2, :], ALU.mult)\
                            .then_inc(inner_done, 1)
                        dve.wait_ge(innerh_done, n + 1)
                        slot = FC * (cs % 2) + t
                        nc.vector.tensor_tensor(mix_l[:, slot, :], tmp[:, 4 + t % 2, :],
                                                mix_h[:, slot, :].bitcast(F32), ALU.subtract)\
                            .then_inc(innerl_done, 1)
                    ahead(gu_slab(c) + i, gu_slab(cs) + i, units_ffn(c, i, False))

            def ahead(s, slot, units):
                if isinstance(s, int) and s + WL >= N_SLABS:
                    return
                low(s + WL, slot + WL, units)

            def y_copy(q):
                dve.wait_ge(yt_done, q + 1)
                nc.vector.tensor_copy(xtok[:, 1, 512 * q:512 * q + 512], mx[:, 1, :]).then_inc(yt_copied_v, 1)

            def down(c, cs):
                for i in range(DN):
                    if i and isinstance(c, int) and c == NCH - 1:
                        y_copy(i - 1)
                    for n in range(4):
                        m = 4 * i + n
                        if not (isinstance(c, int) and c == 0):
                            dve.wait_ge(down_added, 16 * c - 15 + m)
                        dve.wait_ge(unit_done, units_ffn(c, i, True) - 3 + n)
                        nc.vector.tensor_tensor(xT[:, m, :], acc[n][:, 0:T], xT[:, m, :], ALU.add)\
                            .then_inc(down_added, 1)
                    ahead(dn_slab(c) + i, dn_slab(cs) + i, units_ffn(c, i, True))

            ffn_walk(dve, gate_up, down)
            y_copy(3)

        @block.tensor
        def _(pe):
            mm = nc.tensor.matmul

            def x_transpose(k):
                if k >= 4:
                    pe.wait_ge(xt_copied, k - 3)
                for j in range(NTT):
                    rows = P if j < 2 else TS
                    ins = nc.tensor.transpose(mx[:, k % 4, P * j:P * j + rows], xtok[0:rows, j, P * k:P * k + P],
                                              ident[0:rows, 0:rows])
                ins.then_inc(xt_done, 1)

            def spread_rms():
                for j in range(NTT):
                    rows = P if j < 2 else TS
                    pe.wait_ge(diag_made, j + 1)
                    ins = mm(acc[0][:, P * j:P * j + rows], ones[:, :], rms_diag[:, j, 0:rows], start=True, stop=True)
                ins.then_inc(rms_spread, 1)

            for j in range(NTT):
                pe.wait_ge(x_in[j], 16)
            pe.wait_ge(small_in, 16)
            pe.wait_ge(ones_set, 1)
            for k in range(KD):
                x_transpose(k)
                if k == 7:
                    spread_rms()

            def bias_by_distance():
                pe.wait_ge(early_in, 64)
                pe.wait_ge(at_zero, 1)
                mm(mx[0:BH, 3, 0:384], table[:, :], early[0:33, 0:384], start=True, stop=True).then_inc(lut_done, 1)

            def bias_of_rows():
                pe.wait_ge(lut_copied, 1)
                for l in range(LB):
                    mm(mx[:, 2, 0:132], early[0:BH, 384 + P * l:384 + P * l + P], by_dist[:, 127 - l:127 - l + 132],
                       start=(l == 0), stop=(l == LB - 1))
                for l in range(LB):
                    ins = mm(mx[:, 2, 132:133], early[0:BH, 384 + P * l:384 + P * l + P], sink_col,
                             start=(l == 0), stop=(l == LB - 1))
                ins.then_inc(lut_done, 1)

            def passes(bank, slot, k, cols, a_hi, a_lo, between, place=lambda i: i):
                w_h = wh[:, slot % WH, :].rearrange("p (k c) -> p k c", k=k)
                w_l = wl[:, slot % WL, :].rearrange("p (k c) -> p k c", k=k)
                out = acc[bank][:, 0:T]
                for i in range(k):
                    mm(out, w_h[:, i, cols], a_hi[:, place(i), :], start=(i == 0), stop=False)
                    mm(out, w_h[:, i, cols], a_lo[:, place(i), :], start=False, stop=False)
                between()
                for i in range(k):
                    ins = mm(out, w_l[:, i, cols], a_hi[:, place(i), :], start=False, stop=(i == k - 1))
                ins.then_inc(unit_done, 1)

            def passes_as_they_come(bank, slot, high_sem, low_sem, between, place=lambda i: i):
                w_h = wh[:, slot % WH, :].rearrange("p (k c) -> p k c", k=KD)
                w_l = wl[:, slot % WL, :].rearrange("p (k c) -> p k c", k=KD)
                out = acc[bank][:, 0:T]
                for i in range(KD):
                    pe.wait_ge(high_sem, i + 1)
                    mm(out, w_h[:, i, :], act_h[:, place(i), :], start=(i == 0), stop=False)
                between()
                for i in range(KD):
                    mm(out, w_l[:, i, :], act_h[:, place(i), :], start=False, stop=False)
                for i in range(KD):
                    pe.wait_ge(low_sem, i + 1)
                    ins = mm(out, w_h[:, i, :], act_l[:, place(i), :], start=False, stop=(i == KD - 1))
                ins.then_inc(unit_done, 1)

            def qk_squares(i):
                pe.wait_ge(qk_sq, i + 1)
                mm(mx[0:32, 0, 0:T], pair_win[:, 32 - 2 * i:64 - 2 * i], tmp[:, i % 2, :],
                   start=(i == 0), stop=(i == 9)).then_inc(qk_ssq, 1)

            def qk_broadcast():
                pe.wait_ge(rows_low, 1)
                pe.wait_ge(rows_spread, 2)
                for n in range(10):
                    i = KEYS_FIRST[n]
                    if n >= 4:
                        pe.wait_ge(qk_normed, n - 3)
                    mm(mx[:, (1 + n) % 4, 0:T], head_rows[:, P * i:P * i + P], norm_split, start=True, stop=True)\
                        .then_inc(qk_bc, 1)

            def token_major():
                pe.wait_ge(qkv_done, 12)
                pe.wait_ge(qk_normed, 10)
                for c in range(2):
                    for j in range(2):
                        ins = nc.tensor.transpose(mx[:, 0, 256 * j + P * c:256 * j + P * c + P],
                                                  kvT[:, 2 + c, P * j:P * j + P], ident)
                ins.then_inc(vk_t, 1)
                for c in range(2):
                    nc.tensor.transpose(mx[0:TS, 1, P * c:P * c + P], kvT[:, 2 + c, TP:T], ident)
                    nc.tensor.transpose(mx[0:TS, 1, 256 + P * c:256 + P * c + P], kvT[:, c, TP:T], ident)
                    ins = nc.tensor.transpose(mx[:, 2, P * c:P * c + P], kvT[:, c, P:TP], ident)
                ins.then_inc(vk_t, 1)

            def prompt_scores(n):
                k, j = divmod(n, 2)
                width = 2 * WIN if j else WIN
                if n == 0:
                    pe.wait_ge(qk_normed, 10)
                    pe.wait_ge(k_copied, 8)
                    pe.wait_ge(vk_tok, 3)
                else:
                    pe.wait_ge(sc_biased, n)
                for g in range(G):
                    par, gg = g % 2, g // 2
                    half = slice(HD * par, HD * par + HD)
                    ins = mm(mx[:, par, 256 * gg:256 * gg + width], reg_g[half, 2 * k + gg, P * j:P * j + P],
                             k_both[half, k, 0:width], start=True, stop=True)
                ins.then_inc(sc_done, 1)

            def probs_transpose(n):
                j = n % 2
                pe.wait_ge(sc_probs, n + 1)
                if n:
                    if n % 2:
                        pe.wait_ge(mixl_done, n)
                    pe.wait_ge(pt_copied, n)
                else:
                    pe.wait_ge(vk_tok, 3)
                for blk in range(1 - j, 2):
                    for h in range(G):
                        ins = nc.tensor.transpose(mx[:, 2 + blk, P * h:P * h + P],
                                                  scores[:, n % 2, h, P * blk:P * blk + P], ident)
                ins.then_inc(pt_done, 1)

            def prompt_out(n):
                k, j = divmod(n, 2)
                pe.wait_ge(pt_copied, n + 1)
                if n:
                    pe.wait_ge(mixl_done, n)
                for g in range(G):
                    par, gg = g % 2, g // 2
                    for blk in range(1 - j, 2):
                        ins = mm(mx[HD * par:HD * par + HD, 2, P * gg:P * gg + P],
                                 v_tok[:, j - 1 + blk, HD * k:HD * k + HD],
                                 probs_t[:, blk, 2 * par + gg, :], start=(blk == 1 - j), stop=(blk == 1))
                ins.then_inc(pv_done, 1)

            def sampled_scores(i):
                if i == 0:
                    pe.wait_ge(pt_copied, 2 * KVH)
                    pe.wait_ge(mixl_done, 2 * KVH)
                    pe.wait_ge(qr_done, 16)
                    pe.wait_ge(kn_copied, 2)
                else:
                    pe.wait_ge(kc_copied, i)
                    for b in (2 * i - 2, 2 * i - 1):
                        for k in range(KVH):
                            ins = mm(mx[32 * k:32 * k + 32, b // 3, NK * (b % 3):NK * (b % 3) + NK],
                                     q_rows[:, k, b, :], kT_cache[:, b % 2, k // 2, :], start=True, stop=True)
                        ins.then_inc(ss_done, 1)
                if i < NB // 2:
                    pe.wait_ge(kc_in[i % 2], 32 * (i // 2 + 1))
                    for n in range(2):
                        for c in range(2):
                            ins = nc.tensor.transpose(mx[:, 3, 256 * n + P * c:256 * n + P * c + P],
                                                      k_cache[i % 2][:, n, P * c:P * c + P], ident)
                    ins.then_inc(kc_t, 1)

            def sampled_probs():
                pe.wait_ge(ss_probs, 1)
                for n in range(2):
                    for b in range(4 * n, 4 * n + 4):
                        nc.tensor.transpose(mx[:, 2 * n, P * (b % 4):P * (b % 4) + P], s_scores[:, b, 0:WIN], ident)
                        ins = nc.tensor.transpose(mx[0:TS, 2 * n + 1, P * (b % 4):P * (b % 4) + P],
                                                  s_scores[:, b, WIN:NK], ident)
                    ins.then_inc(sp_t, 1)

            def sampled_out():
                pe.wait_ge(sp_copied, 2)
                pe.wait_ge(vc_in, 16)
                out = mx[0:HD, 0, :].rearrange("p (k b m) -> p k b m", k=KVH, b=NB)
                for k in range(KVH):
                    mm(out[:, k], v_tok[0:TS, 2, HD * k:HD * k + HD], s_new_t[:, :, 32 * k:32 * k + 16],
                       start=True, stop=True)
                    for b in range(NB):
                        ins = mm(out[:, k, b], v_cache[:, b, HD * k:HD * k + HD], s_probs_t[:, b, 32 * k:32 * k + 16],
                                 start=False, stop=True, skip_group_check=True)
                ins.then_inc(so_done, 1)

            def level(lv):
                w, ws = (P // 2, TS // 2) if lv else (P, TS)
                if lv:
                    pe.wait_ge(lv_next, lv)
                else:
                    pe.wait_ge(q_made, AH)
                    pe.wait_ge(k_made, AH)
                    pe.wait_ge(so_copied, 2)
                mixer_banks_free(S_LV + lv)
                for b in range(4):
                    if b >= 2 and S_LV + lv > S_SM:
                        pe.wait_ge(s0_new, 2 * (S_LV + lv - S_SM) - 3 + b)
                    if lv:
                        pe.wait_ge(lv_kept, lv_unit(lv - 1, 4 if b == 0 and lv <= 3 else b) + 1)
                    for i in range(4):
                        h, j = 2 * b + i // 2, i % 2
                        q = q_a[:, h, P * j:P * j + P]
                        if lv:
                            q = right_halves(q, LEVELS[lv])
                        ins = mm(mx[:, b, w * i:w * i + w], k_a[:, h, P * j:P * j + P], q, start=True, stop=True)
                    ins.then_inc(lv_done, 1)
                if lv < 3:
                    pe.wait_ge(lv_kept, lv_unit(lv, 0) + 1)
                    for h in range(AH):
                        q = q_a[:, h, TP:T]
                        if lv:
                            q = right_halves(q, LEVELS[lv])
                        ins = mm(mx[0:TS, 0, ws * h:ws * h + ws], k_a[:, h, TP:T], q, start=True, stop=True)
                    ins.then_inc(lv_done, 1)

            def mixer_banks_free(s):
                if s > S_VT:
                    pe.wait_ge(v_tokd, min(s - S_VT, AH))
                if s > S_SM:
                    n = min(s - S_SM, AH)
                    pe.wait_ge(kt_copied, n)
                    pe.wait_ge(sm_oc, n)

            def cross():
                pe.wait_ge(lv_next, 8)
                mixer_banks_free(S_LV + 8)
                for b in range(2):
                    pe.wait_ge(lv_kept, lv_unit(7, b) + 1)
                    for i in range(4):
                        h = 4 * b + i
                        ins = mm(mx[:, b, P * i:P * i + P], k_a[:, h, 0:P], q_a[:, h, P:TP], start=True, stop=True)
                    ins.then_inc(lv_done, 1)

            def levels_kept(s, b):
                if s >= S_LV:
                    n = min(s - S_LV, 8)
                    if n == 8:
                        pe.wait_ge(lv_kept, lv_units_through(7) + 2)
                    elif b == 0 and n < 3:
                        pe.wait_ge(lv_kept, lv_units_through(n))
                    else:
                        pe.wait_ge(lv_kept, lv_unit(n, b) + 1)

            def v_transpose(h):
                levels_kept(S_VT + h, 0)
                pe.wait_ge(i_copied, h + 1)
                for j in range(NTT):
                    rows = P if j < 2 else TS
                    ins = nc.tensor.transpose(mx[0:rows, 0, P * j:P * j + P], iT[:, h % 2, P * j:P * j + rows], ident)
                ins.then_inc(v_t, 1)

            def sampled_head(h):
                levels_kept(S_SM + h, 1)
                if h:
                    pe.wait_ge(sm_oc, h)
                    pe.wait_ge(kt_copied, h)
                nc.tensor.transpose(mx[0:TS, 1, 128:256], k_a[:, h, TP:T], ident)
                pe.wait_ge(v_tokd, h + 1)
                pe.wait_ge(s0_in[h % 2], 16 * (h // 2 + 1))
                mm(mx[:, 1, 0:TS], v_a[0:TS, 2, P * h:P * h + P], a_s[:, h, :], start=True, stop=True)
                for b in range(NB):
                    ins = mm(mx[:, 1, LB * b:LB * b + LB], s0[:, h % 2, b, :], q_a[:, h, TP + LB * b:TP + LB * b + LB],
                             start=False, stop=True, skip_group_check=True)
                ins.then_inc(sm_o, 1)

            def sampled_states(h):
                levels_kept(S_SM + h, 3)
                pe.wait_ge(kt_copied, h + 1)
                pe.wait_ge(v_owned, h + 1)
                if h:
                    pe.wait_ge(s0_new, 2 * h)
                for half in range(2):
                    mm(mx[:, 2 + half, :], kt_s[:, h % 2, :],
                       v_own[:, h % 2, 4 * half:4 * half + 4, :].rearrange("p b v -> p (b v)"),
                       start=True, stop=True).then_inc(sm_st, 1)

            def prompt_head(h):
                if h < 2:
                    pe.wait_ge(lv_kept, lv_units_through(7) + 2)
                    pe.wait_ge(sm_oc, AH)
                    pe.wait_ge(v_tokd, AH)
                else:
                    pe.wait_ge(po_copied, h - 1)
                mm(mx[:, h % 2, 0:P], v_a[:, 0, P * h:P * h + P], a_own[:, h, 0, :], start=True, stop=True)
                mm(mx[:, h % 2, P:TP], v_a[:, 0, P * h:P * h + P], a_cross[:, h, :], start=True, stop=False)
                mm(mx[:, h % 2, P:TP], v_a[:, 1, P * h:P * h + P], a_own[:, h, 1, :], start=False, stop=True)\
                    .then_inc(po_done, 1)

            def prompt_keys(i):
                if i == 0:
                    pe.wait_ge(lv_next, 9)
                    pe.wait_ge(s0_new, 2 * AH)
                else:
                    pe.wait_ge(ps_copied, i)
                for h in (2 * i, 2 * i + 1):
                    for j in range(2):
                        ins = nc.tensor.transpose(mx[:, 2, 256 * (h % 2) + P * j:256 * (h % 2) + P * j + P],
                                                  k_a[:, h, P * j:P * j + P], ident)
                ins.then_inc(ktp_done, 1)

            def prompt_states(i):
                pe.wait_ge(ktp_copied, i + 1)
                for h in (2 * i, 2 * i + 1):
                    for j in range(2):
                        ins = mm(mx[:, 3, P * (h % 2):P * (h % 2) + P], kt_p[:, h % 2, j, :],
                                 v_a[:, j, P * h:P * h + P], start=(j == 0), stop=(j == 1))
                ins.then_inc(ps_done, 1)

            def h_squares(heads):
                pe.wait_ge(po_copied, AH)
                for h in heads:
                    pe.wait_ge(h_sq, h + 1)
                    mm(mx[0:32, 0, 0:T], whole_win[:, 32 - 2 * h:64 - 2 * h], sig[:, h % 2, :],
                       start=(h == 0), stop=(h == AH - 1)).then_inc(h_ssq, 1)

            def h_broadcast(heads):
                pe.wait_ge(h_rows_low, 1)
                pe.wait_ge(h_picked, 2)
                pe.wait_ge(ps_copied, AH // 2)
                for h in heads:
                    if h >= 4:
                        pe.wait_ge(h_normed, h - 3)
                    mm(mx[:, (1 + h) % 4, 0:T], h_pick[:, 2 * h:2 * h + 1].broadcast_to([64, P]), h_split,
                       start=True, stop=True).then_inc(h_bc, 1)

            def x2_ssq():
                pe.wait_ge(sq2_done, 2 * KD - 1)
                mm(mx[:, 0, 0:T], ones[:, :], tmp[:, 0, :], start=True, stop=True).then_inc(ssq2_done, 1)

            def at_start(s):
                if s == S_LUT:
                    bias_by_distance()
                if s == S_LUT + 1:
                    bias_of_rows()
                if s == S_QKN + 1:
                    token_major()
                if 0 <= s - S_AT < 8:
                    prompt_scores(s - S_AT)
                if 0 <= s - S_AT - 2 < 8:
                    prompt_out(s - S_AT - 2)
                if S_SA <= s <= S_SA + 2:
                    sampled_scores(2 * (s - S_SA))
                if s == S_SA + 4:
                    sampled_probs()
                if 0 <= s - S_SM - 1 < AH:
                    sampled_states(s - S_SM - 1)
                if 0 <= s - S_LV < 8:
                    level(s - S_LV)
                if s == S_LV + 8:
                    cross()
                if 0 <= s - S_PO < 4:
                    prompt_head(2 * (s - S_PO))
                    prompt_head(2 * (s - S_PO) + 1)
                if 0 <= s - S_PS < 4:
                    prompt_keys(s - S_PS)
                if s in (S_HN, S_HN + 1):
                    h_squares(range(4 * (s - S_HN), 4 * (s - S_HN) + 2))
                if s == S_HN + 3:
                    h_broadcast(range(4, 6))

            def in_the_middle(s):
                if 2 <= s < 12:
                    qk_squares(s - 2)
                if s == S_QKN:
                    qk_broadcast()
                if 0 <= s - S_AT - 1 < 8:
                    probs_transpose(s - S_AT - 1)
                if S_SA <= s <= S_SA + 1:
                    sampled_scores(2 * (s - S_SA) + 1)
                if s == S_SA + 4:
                    sampled_out()
                if 0 <= s - S_VT < AH:
                    v_transpose(s - S_VT)
                if 0 <= s - S_SM < AH:
                    sampled_head(s - S_SM)
                if 0 <= s - S_PS < 4:
                    prompt_states(s - S_PS)
                if s in (S_HN, S_HN + 1):
                    h_squares(range(4 * (s - S_HN) + 2, 4 * (s - S_HN) + 4))
                if s == S_HN + 2:
                    h_broadcast(range(0, 4))
                if s == S_HN + 3:
                    h_broadcast(range(6, 8))

            def unit_free(u):
                p = u - 4
                if p < 0:
                    if u == 0:
                        pe.wait_ge(rms_copied, 1)
                elif p < S_F:
                    pe.wait_ge(qkv_done, p + 1)
                elif p < S_Q:
                    pe.wait_ge(f_sig, p - S_F + 1)
                elif p < S_I:
                    pe.wait_ge(q_made, p - S_Q + 1)
                elif p < S_G:
                    pe.wait_ge(i_copied, p - S_I + 1)
                elif p < S_O:
                    pe.wait_ge(g_made, p - S_G + 1)
                elif p < U_FFN:
                    pe.wait_ge(x_added, p - U_O + 1)

            for s in range(S_FFN):
                at_start(s)
                pe.wait_ge(high_done, s + 1)

                def low_parts(first):
                    if first:
                        pe.wait_ge(low_done, s + 1)

                if s < S_O:
                    unit_free(s)

                    def between():
                        in_the_middle(s)
                        low_parts(True)

                    if s == 0:
                        passes_as_they_come(0, 0, acth_done, actl_done, between)
                    else:
                        passes(s % 4, s, KD, slice(0, P), act_h, act_l, between)
                else:
                    hgrn = s >= S_O2
                    if s == S_O:
                        pe.wait_ge(mixl_done, 2 * KVH + 1)
                    if s == S_O2:
                        pe.wait_ge(hl_done, AH)
                    for n in range(2):
                        u = U_O + 2 * (s - S_O) + n
                        unit_free(u)
                        a_hi, a_lo = (act_h, act_l) if hgrn else (mix_h, mix_l)
                        passes(u % 4, s, 8, slice(P * n, P * n + P), a_hi, a_lo,
                               lambda: low_parts(n == 0))
                        if n == 0:
                            in_the_middle(s)

            def gate_up(c, cs):
                for i in range(GU):
                    t, up = divmod(i, 2)
                    bank = bank_gu(cs, i)
                    if i >= 4:
                        n = c * FC + (i - 4) // 2
                        pe.wait_ge(inner_done if up else gate_scaled, n + 1)
                    elif isinstance(c, int) and c == 0:
                        pe.wait_ge(x_added, 29 + i)
                    elif isinstance(c, int) and c == 1:
                        pe.wait_ge(inner_done if up else gate_scaled, 2 + i // 2 + 1)
                    else:
                        pe.wait_ge(down_added, 16 * (c - 2) + 12 + i + 1)
                    s = gu_slab(c) + i
                    pe.wait_ge(high_done, s + 1)

                    first = isinstance(c, int) and c == 0 and i == 0

                    def between():
                        if first:
                            x2_ssq()
                        pe.wait_ge(low_done, s + 1)

                    if first:
                        passes_as_they_come(bank, gu_slab(cs), xgh_done, xgl_done, between, x2_place)
                    else:
                        passes(bank, gu_slab(cs) + i, KD, slice(0, P), act_h, act_l, between, x2_place)

            def y_group(q):
                pe.wait_ge(down_added, 16 * (NCH - 1) + 4 * q + 4)
                if q:
                    pe.wait_ge(yt_copied_a, 2 * q)
                    pe.wait_ge(yt_copied_v, q)
                for j in range(NTT):
                    rows = P if j < 2 else TS
                    for i in range(4):
                        ins = nc.tensor.transpose(mx[0:rows, j, P * i:P * i + P], xT[:, 4 * q + i, P * j:P * j + rows],
                                                  ident)
                ins.then_inc(yt_done, 1)

            def down(c, cs):
                half = FC * (cs % 2)
                pe.wait_ge(innerl_done, FC * c + FC)
                for i in range(DN):
                    s = dn_slab(c) + i
                    pe.wait_ge(high_done, s + 1)
                    for n in range(4):
                        m = 4 * i + n
                        if m >= 4:
                            pe.wait_ge(down_added, 16 * c + m - 3)
                        elif isinstance(c, int) and c == NCH - 1:
                            pe.wait_ge(down_added, 16 * (c - 1) + 12 + n + 1)
                        else:
                            pe.wait_ge(inner_done if n % 2 else gate_scaled, (c + 1) * FC + 2 + n // 2 + 1)
                        passes(n, dn_slab(cs) + i, FC, slice(P * n, P * n + P), mix_h[:, half:half + FC, :],
                               mix_l[:, half:half + FC, :],
                               lambda: pe.wait_ge(low_done, s + 1) if n == 0 else None)
                        if n == 1 and i and isinstance(c, int) and c == NCH - 1:
                            y_group(i - 1)

            ffn_walk(pe, gate_up, down)
            y_group(3)


def bank_gu(c, i):
    return i % 4


def right_halves(a, n):
    return a.rearrange("p (b two n) -> p b two n", two=2, n=n)[:, :, 1, :]


def blocks_of(a, n):
    return a.rearrange("p (b n) -> p b n", n=n)


def x2_place(m):
    return (m + 8) % KD


def lv_unit(lv, b):
    return 4 * lv + min(lv, 3) + b


def lv_units_through(lv):
    return lv_unit(lv + 1, 0)


_INS = ['x_prompt', 'x_sample', 'cache_k', 'cache_v', 'state_hgrn', 'norm_mix', 'w_in', 'lower_bounds', 'hgrn_norm',
        'q_norm', 'k_norm', 'attn_sinks', 'rel_bias_table', 'w_out', 'norm_ffn', 'w_gate', 'w_up', 'w_down']
_OUTS = [(1, TP, D), (NB, LB, D), (1, 1, WIN, KVH, HD), (1, 1, WIN, KVH, HD), (1, 1, AH, P, P),
         (1, NB, WIN, KVH, HD), (1, NB, WIN, KVH, HD), (1, NB, AH, P, P)]


def kernel(**inputs):
    import numpy as _np
    import concourse.bacc as _bacc
    from concourse import mybir as _mybir
    from concourse.bass_utils import run_bass_kernel_spmd as _run

    nc = _bacc.Bacc("TRN2", target_bir_lowering=False, num_devices=1)
    arrays, args = {}, []
    for name in _INS:
        a = _np.ascontiguousarray(inputs[name])
        arrays[f"in_{name}_dram"] = a
        args.append(nc.dram_tensor(f"in_{name}_dram", a.shape, _mybir.dt.from_np(a.dtype), kind="ExternalInput").ap())
    for name, a in zip(("small", "masks", "early"), constants()):
        arrays[f"const_{name}_dram"] = a
        args.append(nc.dram_tensor(f"const_{name}_dram", a.shape, _mybir.dt.from_np(a.dtype), kind="ExternalInput").ap())
    for i, shape in enumerate(_OUTS):
        args.append(nc.dram_tensor(f"out_{i}_dram", shape, F32, kind="ExternalOutput").ap())
    layer_kernel(nc, *args)
    r = _run(nc, [arrays], core_ids=[0])
    return tuple(r.results[0][f"out_{i}_dram"] for i in range(len(_OUTS)))
```
